# Optimizing a Trainium2 kernel written in Bass

```python
import math
import jax, jax.numpy as jnp
from jax import lax
import numpy as np

D_MODEL = 1024
BATCH = 1
SEQ = 1024
DEPTH = 2

H_DN = 4
DK_DN = 128
DV_DN = 128
DN_CONV = 4
DN_CHUNK = 64
H_FOX = 4
D_FOX = 128
D_DIFF = 64
H_DIFF = D_MODEL // (2 * D_DIFF)
ROPE_THETA = 10000.0
Q_BLOCK = 128
D_FF = 128 * ((8 * D_MODEL // 3 + 127) // 128)
FFN_CONV = 3
EPS = 1e-6

N_EVEN = (DEPTH + 1) // 2
N_ODD = DEPTH // 2
DN_QKV = H_DN * (2 * DK_DN + DV_DN)
EV_SIZES = (DN_QKV, H_DN * DV_DN, H_DN, H_DN, H_FOX * D_FOX, H_FOX * D_FOX, H_FOX * D_FOX, H_FOX)
EV_IN = DN_QKV + H_DN * DV_DN + 2 * H_DN + 3 * H_FOX * D_FOX + H_FOX
OD_IN = 3 * D_MODEL

kernel_name = 'hybrid_deltanet_fox_diffattn_convffn'

def _rmsnorm(x, w):
    xf = x.astype(jnp.float32)
    y = xf * lax.rsqrt(jnp.mean(xf * xf, axis=-1, keepdims=True) + EPS)
    return (y * w.astype(jnp.float32)).astype(x.dtype)

def _l2norm(x):
    xf = x.astype(jnp.float32)
    return (xf * lax.rsqrt(jnp.sum(xf * xf, axis=-1, keepdims=True) + EPS)).astype(x.dtype)

def _split_cols(x, sizes):
    out, start = [], 0
    for n in sizes:
        out.append(x[..., start:start + n])
        start += n
    return out

def _causal_dwconv(x, w):
    k, c = w.shape
    return lax.conv_general_dilated(x, w[:, None, :], window_strides=(1,), padding=[(k - 1, 0)],
                                    dimension_numbers=('NWC', 'WIO', 'NWC'), feature_group_count=c)

def _rope(x, pos):
    d = x.shape[-1]
    half = d // 2
    inv = 1.0 / (ROPE_THETA ** (jnp.arange(half, dtype=jnp.float32) * 2.0 / d))
    ang = pos[:, None] * inv[None, :]
    cos, sin = jnp.cos(ang), jnp.sin(ang)
    xf = x.astype(jnp.float32)
    x1, x2 = xf[..., :half], xf[..., half:]
    return jnp.concatenate([x1 * cos - x2 * sin, x1 * sin + x2 * cos], axis=-1).astype(x.dtype)

def _gated_delta_rule(q, k, v, g, beta):
    out_dtype = v.dtype
    f32 = jnp.float32
    b, h, s, dk = q.shape
    dv = v.shape[-1]
    c = DN_CHUNK
    n = s // c
    q = q.astype(f32) * dk ** -0.5
    k, v, g, beta = k.astype(f32), v.astype(f32), g.astype(f32), beta.astype(f32)
    chunk = lambda t: t.reshape(b, h, n, c, *t.shape[3:])
    q, k, v, g, beta = chunk(q), chunk(k), chunk(v), chunk(g), chunk(beta)
    kb = k * beta[..., None]
    vb = v * beta[..., None]
    g = jnp.cumsum(g, axis=-1)
    incl = jnp.tril(jnp.ones((c, c), dtype=bool))
    strict = jnp.tril(jnp.ones((c, c), dtype=bool), -1)
    gdiff = g[..., :, None] - g[..., None, :]
    decay = jnp.where(incl, jnp.exp(jnp.where(incl, gdiff, 0.0)), 0.0)
    lower = jnp.where(strict, jnp.einsum('bhncd,bhnsd->bhncs', kb, k) * decay, 0.0)
    t_mat = lower + jnp.eye(c, dtype=f32)
    u = lax.linalg.triangular_solve(t_mat, vb, left_side=True, lower=True, unit_diagonal=True)
    w = lax.linalg.triangular_solve(t_mat, kb * jnp.exp(g)[..., None], left_side=True, lower=True,
                                    unit_diagonal=True)
    qk = jnp.einsum('bhncd,bhnsd->bhncs', q, k) * decay
    qg = q * jnp.exp(g)[..., None]
    kd = k * jnp.exp(g[..., -1:] - g)[..., None]
    g_last = jnp.exp(g[..., -1])

    def step(state, xs):
        u_c, w_c, qk_c, qg_c, kd_c, gl_c = xs
        v_new = u_c - jnp.einsum('bhck,bhkv->bhcv', w_c, state)
        o_c = jnp.einsum('bhck,bhkv->bhcv', qg_c, state) + jnp.einsum('bhcs,bhsv->bhcv', qk_c, v_new)
        state = state * gl_c[..., None, None] + jnp.einsum('bhck,bhcv->bhkv', kd_c, v_new)
        return state, o_c

    lead = lambda t: jnp.moveaxis(t, 2, 0)
    s0 = jnp.zeros((b, h, dk, dv), f32)
    _, o = lax.scan(step, s0, (lead(u), lead(w), lead(qk), lead(qg), lead(kd), lead(g_last)))
    o = jnp.moveaxis(o, 0, 2).reshape(b, h, s, dv)
    return o.astype(out_dtype)

def _fox_attention(q, k, v, c):
    b, h, s, d = q.shape
    nb = s // Q_BLOCK
    scale = d ** -0.5
    kpos = jnp.arange(s)

    def blk(i):
        start = i * Q_BLOCK
        qb = lax.dynamic_slice_in_dim(q, start, Q_BLOCK, axis=2)
        cb = lax.dynamic_slice_in_dim(c, start, Q_BLOCK, axis=2)
        logits = (jnp.einsum('bhqd,bhkd->bhqk', qb, k).astype(jnp.float32) * scale
                  + cb[..., :, None] - c[..., None, :])
        qpos = start + jnp.arange(Q_BLOCK)
        logits = jnp.where(kpos[None, :] <= qpos[:, None], logits, -jnp.inf)
        p = jax.nn.softmax(logits, axis=-1)
        return jnp.einsum('bhqk,bhkd->bhqd', p.astype(v.dtype), v)

    o = lax.map(blk, jnp.arange(nb))
    return jnp.moveaxis(o, 0, 2).reshape(b, h, s, d)

def _diff_attention(q, k, v, lam):
    b, h, _, s, dh = q.shape
    nb = s // Q_BLOCK
    scale = dh ** -0.5
    kpos = jnp.arange(s)

    def blk(i):
        start = i * Q_BLOCK
        qb = lax.dynamic_slice_in_dim(q, start, Q_BLOCK, axis=3)
        logits = jnp.einsum('bhmqd,bhmkd->bhmqk', qb, k).astype(jnp.float32) * scale
        qpos = start + jnp.arange(Q_BLOCK)
        logits = jnp.where(kpos[None, :] <= qpos[:, None], logits, -jnp.inf)
        p = jax.nn.softmax(logits, axis=-1)
        pd = p[:, :, 0] - lam * p[:, :, 1]
        return jnp.einsum('bhqk,bhkd->bhqd', pd.astype(v.dtype), v)

    o = lax.map(blk, jnp.arange(nb))
    return jnp.moveaxis(o, 0, 2).reshape(b, h, s, v.shape[-1])

def _deltanet_fox_mixer(hn, w_in, conv_w, a_log, dt_bias, dn_norm_w, f_bias, w_out):
    b, s, _ = hn.shape
    f32 = jnp.float32
    proj = hn @ w_in
    qkv_dn, z_dn, beta_lg, a_lg, q_f, k_f, v_f, f_lg = _split_cols(proj, EV_SIZES)
    heads = lambda t, nh: t.reshape(b, s, nh, -1).transpose(0, 2, 1, 3)
    qkv_dn = jax.nn.silu(_causal_dwconv(qkv_dn, conv_w))
    q_d, k_d, v_d = _split_cols(qkv_dn, (H_DN * DK_DN, H_DN * DK_DN, H_DN * DV_DN))
    q_d = _l2norm(heads(q_d, H_DN))
    k_d = _l2norm(heads(k_d, H_DN))
    v_d = heads(v_d, H_DN)
    beta = jax.nn.sigmoid(beta_lg.astype(f32)).transpose(0, 2, 1)
    g = (-jnp.exp(a_log.astype(f32))
         * jax.nn.softplus(a_lg.astype(f32) + dt_bias.astype(f32))).transpose(0, 2, 1)
    o_d = _gated_delta_rule(q_d, k_d, v_d, g, beta).transpose(0, 2, 1, 3)
    o_d = _rmsnorm(o_d, dn_norm_w) * jax.nn.silu(z_dn.reshape(b, s, H_DN, DV_DN))
    log_f = jax.nn.log_sigmoid(f_lg.astype(f32) + f_bias.astype(f32))
    c = jnp.cumsum(log_f, axis=1).transpose(0, 2, 1)
    o_f = _fox_attention(heads(q_f, H_FOX), heads(k_f, H_FOX), heads(v_f, H_FOX), c)
    o_f = o_f.transpose(0, 2, 1, 3).reshape(b, s, H_FOX * D_FOX)
    o = jnp.concatenate([o_d.reshape(b, s, H_DN * DV_DN).astype(o_f.dtype), o_f], axis=-1)
    return o @ w_out

def _diff_mixer(hn, w_in, lam_vecs, subln_w, w_out, lambda_init):
    b, s, _ = hn.shape
    q, k, v = _split_cols(hn @ w_in, (D_MODEL, D_MODEL, D_MODEL))
    q = q.reshape(b, s, H_DIFF, 2, D_DIFF).transpose(0, 2, 3, 1, 4)
    k = k.reshape(b, s, H_DIFF, 2, D_DIFF).transpose(0, 2, 3, 1, 4)
    v = v.reshape(b, s, H_DIFF, 2 * D_DIFF).transpose(0, 2, 1, 3)
    pos = jnp.arange(s, dtype=jnp.float32)
    q = _rope(q, pos)
    k = _rope(k, pos)
    lv = lam_vecs.astype(jnp.float32)
    lam = jnp.exp(jnp.sum(lv[0] * lv[1])) - jnp.exp(jnp.sum(lv[2] * lv[3])) + lambda_init
    o = _diff_attention(q, k, v, lam)
    o = _rmsnorm(o, subln_w) * (1.0 - lambda_init)
    o = o.transpose(0, 2, 1, 3).reshape(b, s, D_MODEL)
    return o @ w_out

def _conv_ffn(hn, w_up, conv_w, conv_b, w_down):
    gate, val = _split_cols(hn @ w_up, (D_FF, D_FF))
    gate = _causal_dwconv(gate, conv_w) + conv_b
    return (jax.nn.silu(gate) * val) @ w_down

def setup_inputs(seed: int = 0) -> dict:
    key = jax.random.key(seed)
    ks = jax.random.split(key, 20)
    f32 = jnp.float32
    nrm = lambda kk, shape, scale: jax.random.normal(kk, shape, f32) * scale
    dt = jnp.exp(jax.random.uniform(ks[5], (N_EVEN, H_DN), f32, math.log(1e-3), math.log(1e-1)))
    return {
        'x': nrm(ks[0], (BATCH, SEQ, D_MODEL), 1.0),
        'ev_norm_w': 1.0 + nrm(ks[1], (N_EVEN, D_MODEL), 0.02),
        'ev_w_in': nrm(ks[2], (N_EVEN, D_MODEL, EV_IN), D_MODEL ** -0.5),
        'dn_conv_w': nrm(ks[3], (N_EVEN, DN_CONV, DN_QKV), DN_CONV ** -0.5),
        'dn_a_log': jnp.log(jax.random.uniform(ks[4], (N_EVEN, H_DN), f32, 1.0, 16.0)),
        'dn_dt_bias': dt + jnp.log(-jnp.expm1(-dt)),
        'dn_norm_w': 1.0 + nrm(ks[6], (N_EVEN, DV_DN), 0.02),
        'fox_f_bias': 2.0 + nrm(ks[7], (N_EVEN, H_FOX), 0.5),
        'ev_w_out': nrm(ks[8], (N_EVEN, D_MODEL, D_MODEL), D_MODEL ** -0.5),
        'od_norm_w': 1.0 + nrm(ks[9], (N_ODD, D_MODEL), 0.02),
        'od_w_in': nrm(ks[10], (N_ODD, D_MODEL, OD_IN), D_MODEL ** -0.5),
        'diff_lambda': nrm(ks[11], (N_ODD, 4, D_DIFF), 0.1),
        'diff_subln_w': 1.0 + nrm(ks[12], (N_ODD, 2 * D_DIFF), 0.02),
        'od_w_out': nrm(ks[13], (N_ODD, D_MODEL, D_MODEL), D_MODEL ** -0.5),
        'ffn_norm_w': 1.0 + nrm(ks[14], (DEPTH, D_MODEL), 0.02),
        'ffn_w_up': nrm(ks[15], (DEPTH, D_MODEL, 2 * D_FF), D_MODEL ** -0.5),
        'ffn_conv_w': nrm(ks[16], (DEPTH, FFN_CONV, D_FF), FFN_CONV ** -0.5),
        'ffn_conv_b': nrm(ks[17], (DEPTH, D_FF), 0.02),
        'ffn_w_down': nrm(ks[18], (DEPTH, D_FF, D_MODEL), D_FF ** -0.5),
        'final_norm_w': 1.0 + nrm(ks[19], (D_MODEL,), 0.02),
    }

def reference(x, ev_norm_w, ev_w_in, dn_conv_w, dn_a_log, dn_dt_bias, dn_norm_w, fox_f_bias, ev_w_out,
              od_norm_w, od_w_in, diff_lambda, diff_subln_w, od_w_out,
              ffn_norm_w, ffn_w_up, ffn_conv_w, ffn_conv_b, ffn_w_down, final_norm_w):
    for i in range(DEPTH):
        j = i // 2
        if i % 2 == 0:
            x = x + _deltanet_fox_mixer(_rmsnorm(x, ev_norm_w[j]), ev_w_in[j], dn_conv_w[j], dn_a_log[j],
                                        dn_dt_bias[j], dn_norm_w[j], fox_f_bias[j], ev_w_out[j])
        else:
            lambda_init = 0.8 - 0.6 * math.exp(-0.3 * i)
            x = x + _diff_mixer(_rmsnorm(x, od_norm_w[j]), od_w_in[j], diff_lambda[j], diff_subln_w[j],
                                od_w_out[j], lambda_init)
        x = x + _conv_ffn(_rmsnorm(x, ffn_norm_w[i]), ffn_w_up[i], ffn_conv_w[i], ffn_conv_b[i], ffn_w_down[i])
    return _rmsnorm(x, final_norm_w)


_drawn_inputs = setup_inputs


def setup_inputs(seed=0):
    import zlib

    import numpy as np

    out = dict(_drawn_inputs(seed))
    spreads = {}
    factors = {'dn_norm_w': 5.028,
     'od_norm_w': 3.233,
     'diff_subln_w': 6.279,
     'ffn_norm_w': 2.696,
     'ffn_conv_b': 4.001,
     'final_norm_w': 2.837}
    for name, (base, spread) in spreads.items():
        noise = np.random.default_rng([zlib.crc32(name.encode()), seed]).standard_normal(out[name].shape)
        drawn = base * np.exp(spread * noise) if base else spread * noise
        out[name] = __import__('jax').numpy.asarray(drawn.astype(out[name].dtype))
    for name, factor in factors.items():
        out[name] = (out[name] * factor).astype(out[name].dtype)
    return out
```

```python
from contextlib import ExitStack

import numpy as np

import concourse.bass as bass
from concourse import mybir

F32, F32R, BF16 = mybir.dt.float32, mybir.dt.float32r, mybir.dt.bfloat16
ALU, ACT, AX = mybir.AluOpType, mybir.ActivationFunctionType, mybir.AxisListType

P = 128
D = 1024
S = 1024
KT = D // P
NT = S // P
HALF = 512
H_DN, H_FOX, H_DIFF = 4, 4, 8
DH = 64
CHUNK = 64
FF = 2816
FT = FF // P
GROUPS = FT // 2
EPS = 1e-6
NEG = -1e30
LAMBDA_INIT = 0.8 - 0.6 * float(np.exp(-0.3))

B_SMALL = 0
B_DN = 1
B_Z = B_DN + 3 * H_DN
B_FOX = B_Z + H_DN
B_EVOUT = B_FOX + 3 * H_FOX
B_FFN0 = B_EVOUT + KT
B_DIFF = B_FFN0 + 3 * FT
B_ODOUT = B_DIFF + 3 * H_DIFF
B_FFN1 = B_ODOUT + KT
N_BLOCKS = B_FFN1 + 3 * FT
RING = 3
assert N_BLOCKS % RING == 0

C_NORM = 0
C_DNCONV = C_NORM + 5 * KT
C_FFN = C_DNCONV + 12 * 4
C_DNW = C_FFN + 2 * FT * 4
C_SUBLN = C_DNW + 1
C_LAM = C_SUBLN + 1
C_ROW = C_LAM + 4 * DH
N_COLS = C_ROW + 3

R_BETA, R_G, R_F, R_TAIL = 0, 32, 64, 96
LEVELS = 6


SHARE = (17, 17, 17, 17, 16, 16, 16, 16, 12)
assert sum(SHARE) == 144
HALVES_DONE = [[j for j in range(6) if sum(SHARE[:n]) < 24 * (j + 1) <= sum(SHARE[:n + 1])] for n in range(9)]
assert all(len(x) < 2 for x in HALVES_DONE)
rounds = lambda tile: 2 + tile + max(0, tile - 4)


class Chain:

    def __init__(self, engine, sem):
        self.engine, self.sem, self.start, self.n = engine, sem, 0, 0

    def __call__(self, instruction):
        instruction.then_inc(self.sem, 1)
        self.n += 1
        self.engine.wait_ge(self.sem, self.start + self.n)

    def enter(self, i, per, first=0):
        self.outer, self.per = self.start + self.n, per
        self.start, self.n = i * per + (self.outer - first * per), 0

    def leave(self, count):
        assert self.n == self.per, f"{self.engine}: {self.n} links in the body, not {self.per}"
        self.start, self.n = self.outer + count * self.per, 0


def build(nc, t, debug=None):
    with ExitStack() as ctx:
        sb = lambda name, shape, dt=F32: ctx.enter_context(nc.sbuf_tensor(name, shape, dt))

        X = sb("X", [P, KT, S])
        HNH = sb("HNH", [P, KT, S], F32R)
        HNL = sb("HNL", [P, KT, S], F32R)
        WRAW = sb("WRAW", [P, RING, D])
        WH = sb("WH", [P, RING, D], F32R)
        WL = sb("WL", [P, RING, D], F32R)
        ident = sb("ident", [P, P])
        ones = sb("ones", [P, P])
        cols = sb("cols", [P, N_COLS])
        epsc = sb("epsc", [P, 1])
        small = sb("small", [P, 64])
        identb = sb("identb", [P, P], BF16)
        maskb = sb("maskb", [P, P], BF16)

        def stage(**shapes):
            with ExitStack() as own:
                return {n: own.enter_context(nc.sbuf_tensor(n, s, d)) for n, (s, d) in shapes.items()}

        even = ExitStack()
        CHL = even.enter_context(nc.sbuf_tensor("CHL", [P, S], F32R))
        row = ([P, S], F32)
        row_r = ([P, S], F32R)
        dnp = stage(dn_conv=([P, 2, S], F32), dn_out=([P, 2, S], F32), lg=row, lg_a=row, lg_b=row, rst=row)
        four = ([P, 4, P], F32)
        dn = stage(
            SC=row, TE=([P, NT, P], F32), TKN=([P, NT, P], F32), GLB=([P, 4, 16], F32), SELG=([P, 4, P], F32),
            LM=([P, LEVELS, P], F32), MI=([P, P], F32), te=([P, P], F32), tkn=([P, P], F32), glt=([P, 4, 2], F32),
            qs=four, ks=four, vs=four, sq=four, kn=four, kb=four, qn=four, qg=four, kbg=four, kd=four, vb=four,
            knT=four, kbqT=([P, 4, 2, P], F32), qgT=four, dec=four, QKT=four, LT=four, u=four, wT=four, vn=four,
            St=four, on=four,
        )
        zst = stage(z_gate=([P, 2, S], F32))
        att = dict(
            rawq=row, rawk=row, rawv=row, QH=row_r, QL=row_r, KH=row_r, KL=row_r,
            VH=([P, NT, P], F32R), VL=([P, NT, P], F32R), PTH=([P, NT, P], F32R), PTL=([P, NT, P], F32R),
            e0=([P, 2, S], F32), ot=([P, P], F32), sums=([P, 2, 2], F32), nmax=([P, 2], F32), rinv=([P, 4], F32),
        )
        fox = stage(**{f"f_{k}": v for k, v in att.items()}, SELC=([P, 4, P], F32), selc=([P, P], F32R))
        even.close()
        dif = stage(**{f"d_{k}": v for k, v in att.items()}, e1=row, xs=row, cosT=row, sinT=row,
                    sqd=([P, P], F32), dsc=([P, 8], F32))
        ost = stage(xt=([P, 2, S], F32))
        ffn = stage(
            HH=([P, 4, S], F32R), HL=([P, 4, S], F32R), cv=([P, 2, S], F32), hb=([P, S], F32), fp=([P, 2, 4], F32),
            sqb=([P, 2, S], F32), acc=row, rt=row,
        )
        sqb, acc, rt = ffn["sqb"], ffn["acc"], ffn["rt"]
        cv = ffn["cv"]

        ps = ctx.enter_context(nc.psum_tensor("ps", [P, 8, HALF], F32))
        bank = lambda b, n=1: ps[:, b:b + n, :].rearrange("p b c -> p (b c)")

        names = (
            "consts_in x_in spilled w_split w_split_hi blocks_freed first_half small_consts "
            "sq_done sq_added sum_ready root_ready hn_scaled hn_hi hn_ready out_scaled out_sent out_w "
            "pe_chain act_chain dve_chain stage_end "
            "conv_start conv_taps dn_silu rows_in rows_y rows_abs rows_l rows_scan rows_turned rows_kept "
            "rows_tail glb_ready te_ready chl_ready "
            "dn_loaded dn_staged dn_turn1 dn_square dn_ss dn_root dn_scale dn_turn2 dn_evac2 dn_pair dn_dec dn_exp dn_mask "
            "dn_x1t dn_x1 dn_lts dn_y dn_yc dn_p dn_xc dn_uw dn_uc dn_wc dn_ws dn_vn dn_o dn_s dn_sc dn_osq dn_oss "
            "dn_ort dn_on dn_ot dn_ow z_silu z_done "
            "o_hi o_split x_back xt_free out_added "
            "gate_mid gate_taps silu_done gated hid_hi hid_lo params_in down_ready down_added "
        ).split()
        sem = {n: ctx.enter_context(nc.semaphore(n)) for n in names}
        w_loaded = [ctx.enter_context(nc.semaphore(f"w_loaded{i}")) for i in range(RING)]
        dn_stored = [ctx.enter_context(nc.semaphore(f"dn_stored{i}")) for i in range(2)]
        for kind in "fd":
            for n in ("raw_written swapped_q swapped_k roped qk_hi qk_lo turned turn_hi turn_lo scored max_ready exped "
                      "combined pv_done squared ss_ready rootd o_scaled o_turned o_written sel_ready").split():
                sem[f"{kind}_{n}"] = ctx.enter_context(nc.semaphore(f"{kind}_{n}"))
        s = sem
        block = ctx.enter_context(nc.Block())

        col = lambda c, n=1: cols[:, c:c + n]

        @block.sync
        def _(sp):
            def load(b, slot, turn):
                sp.dma_start(WRAW[:, slot, :], t["w"][b, :, :]).then_inc(w_loaded[slot], 16)

            for b in range(RING):
                load(b, b, 0)
            with sp.Fori(1, N_BLOCKS // RING) as i:
                for slot in range(RING):
                    sp.wait_ge(s["w_split"], i * RING + slot - RING + 1)
                    load(i * RING + slot, slot, i)

        @block.gpsimd
        def _(pool):
            def split(b, slot, turn):
                pool.wait_ge(w_loaded[slot], turn * 16 + 16)
                pool.tensor_tensor(WH[:, slot, :], WRAW[:, slot, :], ones[:, 0:1].to_broadcast([P, D]), ALU.mult).then_inc(
                    s["w_split_hi"], 1)
                pool.wait_ge(s["w_split_hi"], b + 1)
                pool.tensor_tensor(WL[:, slot, :], WRAW[:, slot, :], WH[:, slot, :], ALU.subtract).then_inc(
                    s["w_split"], 1)

            pool.wait_ge(s["small_consts"], 1)
            for b in range(RING):
                split(b, b, 0)
            with pool.Fori(1, N_BLOCKS // RING) as i:
                for slot in range(RING):
                    pool.wait_ge(s["blocks_freed"], i * RING + slot - RING + 1)
                    split(i * RING + slot, slot, i)

        def stage_end(eng, n):
            eng.drain().then_inc(s["stage_end"], 1)
            eng.wait_ge(s["stage_end"], 3 * n)

        @block.tensor
        def _(pe):
            def split_product(out, wh, wl, xh, xl, first, last):
                pe.matmul(out, wh, xh, start=first, stop=False)
                pe.matmul(out, wh, xl, start=False, stop=False)
                return pe.matmul(out, wl, xh, start=False, stop=last)

            def project(b, slot, half, out, ks=range(KT), first_norm=None):
                if half == 0 and ks[0] == 0:
                    pe.wait_ge(s["w_split"], b + 1)
                for k in ks:
                    if first_norm is not None:
                        pe.wait_ge(s["hn_ready"], 8 * first_norm + k + 1)
                    cs, ts = slice(k * P, k * P + P), slice(half * HALF, half * HALF + HALF)
                    mm = split_product(out, WH[:, slot, cs], WL[:, slot, cs], HNH[:, k, ts], HNL[:, k, ts],
                                       k == 0, k == KT - 1)
                if ks[-1] == KT - 1:
                    mm.then_inc(s["first_half"] if half == 0 else s["blocks_freed"], 1)

            def norm(n):
                pe.wait_ge(s["sq_added"], 8 * n + 8)
                for h in range(2):
                    mm = pe.matmul(bank(6 + h), ones[:, :], acc[:, h * HALF:h * HALF + HALF], start=True, stop=True)
                mm.then_inc(s["sum_ready"], 1)

            pe.wait_ge(s["small_consts"], 1)
            pe.wait_ge(s["consts_in"], 16)
            norm(0)
            for n in range(13):
                b = B_SMALL + n
                if n >= 2:
                    pe.wait_ge(s["conv_taps"], n - 1)
                for half in range(2):
                    project(b, b % RING, half, bank(2 * (n % 2) + half), first_norm=0 if n == 0 else None)
            pe.wait_ge(s["rows_scan"], 2)
            pe.wait_ge(s["rows_in"], 48)
            for r in range(2):
                if r:
                    pe.wait_ge(s["rows_kept"], 1)
                for j in range(4):
                    tr = pe.transpose(bank(4)[:, j * P:j * P + P], dn["SC"][:, (4 * r + j) * P:(4 * r + j + 1) * P],
                                      ident[:, :])
                tr.then_inc(s["rows_turned"], 1)
            for h in range(4):
                mm = pe.matmul(bank(5)[:, h * 16:h * 16 + 16], dn["SELG"][:, h, :],
                               dn["SC"][:, CHUNK - 1:S:CHUNK], start=True, stop=True)
            mm.then_inc(s["rows_turned"], 1)
            stage_end(pe, 1)

            d = dn

            def turn4(bk, src, name=None):
                for h in range(4):
                    tr = pe.transpose(bank(bk)[:, h * P:h * P + P], src[:, h, :], ident[:, :])
                return tr

            with pe.Fori(0, NT) as i:
                pe.wait_ge(s["dn_loaded"], 48 * i + 48)
                pe.wait_ge(s["dn_sc"], 8 * i + 4)
                turn4(2, d["ks"])
                turn4(3, d["qs"])
                turn4(4, d["vs"]).then_inc(s["dn_turn1"], 1)
                pe.wait_ge(s["dn_scale"], 7 * i + 2)
                turn4(5, d["kn"]).then_inc(s["dn_turn2"], 1)
                turn4(6, d["kb"]).then_inc(s["dn_turn2"], 1)
                pe.wait_ge(s["dn_scale"], 7 * i + 4)
                turn4(7, d["qn"]).then_inc(s["dn_turn2"], 1)
                pe.wait_ge(s["dn_scale"], 7 * i + 7)
                turn4(2, d["qg"]).then_inc(s["dn_turn2"], 1)
                pe.wait_ge(s["dn_evac2"], 4 * i + 4)
                for h in range(4):
                    mm = pe.matmul(bank(3 + h // 2)[:, (h % 2) * 2 * P:(h % 2 + 1) * 2 * P], d["knT"][:, h, :],
                                   d["kbqT"][:, h, :, :].rearrange("p a c -> p (a c)"), start=True, stop=True)
                mm.then_inc(s["dn_pair"], 1)
                for h in range(4):
                    mm = pe.matmul(bank(5)[:, h * P:h * P + P], d["SELG"][:, h, :], d["SC"][:, bass.ts(i, P)],
                                   start=True, stop=True)
                mm.then_inc(s["dn_pair"], 1)
                pe.wait_ge(s["dn_lts"], LEVELS * i + 1)
                turn4(6, d["kn"]).then_inc(s["dn_x1t"], 1)
                for lv in range(1, LEVELS):
                    pe.wait_ge(s["dn_lts"], LEVELS * i + lv + 1)
                    pe.wait_ge(s["dn_xc"], 11 * i + 2 * lv)
                    for h in range(4):
                        mm = pe.matmul(bank(7)[:, h * P:h * P + P], d[["kn", "kb"][lv % 2]][:, h, :], d["qs"][:, h, :],
                                       start=True, stop=True)
                    mm.then_inc(s["dn_y"], 1)
                    pe.wait_ge(s["dn_yc"], (LEVELS - 1) * i + lv)
                    for h in range(4):
                        mm = pe.matmul(bank(2)[:, h * P:h * P + P], d["sq"][:, h, :], d["vs"][:, h, :],
                                       start=True, stop=True)
                    mm.then_inc(s["dn_p"], 1)
                    if lv < LEVELS - 1:
                        for h in range(4):
                            mm = pe.matmul(bank(5)[:, h * P:h * P + P], d["vs"][:, h, :], d["sq"][:, h, :],
                                           start=True, stop=True)
                        mm.then_inc(s["dn_p"], 1)
                pe.wait_ge(s["dn_xc"], 11 * i + 11)
                for h in range(4):
                    mm = pe.matmul(bank(3)[:, h * P:h * P + P], d["vs"][:, h, :], d["vb"][:, h, :], start=True, stop=True)
                mm.then_inc(s["dn_uw"], 1)
                for h in range(4):
                    mm = pe.matmul(bank(4)[:, h * P:h * P + P], d["kbg"][:, h, :], d["vs"][:, h, :], start=True, stop=True)
                mm.then_inc(s["dn_uw"], 1)
                for c in range(2):
                    r = slice(c * CHUNK, c * CHUNK + CHUNK)
                    if c == 0:
                        pe.wait_ge(s["dn_wc"], i + 1)
                        pe.wait_ge(s["dn_sc"], 8 * i + 4)
                    else:
                        pe.wait_ge(s["dn_sc"], 8 * i + 8)
                    for h in range(4):
                        mm = pe.matmul(bank(6)[r, h * P:h * P + P], d["wT"][:, h, r], d["St"][:, h, :],
                                       start=True, stop=True)
                    mm.then_inc(s["dn_ws"], 1)
                    if c == 0:
                        pe.wait_ge(s["dn_mask"], 2 * i + 2)
                    pe.wait_ge(s["dn_vn"], 2 * i + c + 1)
                    for h in range(4):
                        o = bank(7)[r, h * P:h * P + P]
                        pe.matmul(o, d["qgT"][:, h, r], d["St"][:, h, :], start=True, stop=False)
                        mm = pe.matmul(o, d["QKT"][r, h, r], d["vn"][r, h, :], start=False, stop=True)
                    mm.then_inc(s["dn_o"], 1)
                    for h in range(4):
                        mm = pe.matmul(bank(2)[:, h * P:h * P + P], d["kd"][r, h, :], d["vn"][r, h, :],
                                       start=True, stop=True)
                    mm.then_inc(s["dn_s"], 1)
                pe.wait_ge(s["dn_on"], i + 1)
                turn4(5, d["on"]).then_inc(s["dn_ot"], 1)
            stage_end(pe, 2)

            for n in range(H_DN):
                b = B_Z + n
                if n >= 2:
                    pe.wait_ge(s["z_silu"], n - 1)
                for half in range(2):
                    project(b, b % RING, half, bank(2 * (n % 2) + half))
            stage_end(pe, 3)

            def attention(kind, buf, maps, heads, b0, halves_before):
                z = lambda n: s[f"{kind}_{n}"]
                g = lambda n: buf[f"{kind}_{n}"]

                def proj(hp, m0, m1):
                    for m in range(m0, m1):
                        j, k, p = m // 24, m % 24 // 3, m % 3
                        slot, half = (b0 + j // 2) % RING, j % 2
                        if m % 48 == 0:
                            pe.wait_ge(s["w_split"], 3 * hp + (b0 + j // 2 + 1))
                        if m % 24 == 0 and not (isinstance(hp, int) and hp == 0 and j < 2):
                            pe.wait_ge(z("raw_written"), 6 * hp + (j - 1))
                        cs, ts = slice(k * P, k * P + P), slice(half * HALF, half * HALF + HALF)
                        mm = pe.matmul(bank(half), (WL if p == 2 else WH)[:, slot, cs],
                                       (HNL if p == 1 else HNH)[:, k, ts], start=m % 24 == 0, stop=m % 24 == 23)
                        if m % 24 == 23:
                            mm.then_inc(s["first_half"] if half == 0 else s["blocks_freed"], 1)

                def scores(h, tt):
                    n = P * (tt + 1)
                    for m in range(maps):
                        rows = slice(0, P) if maps == 1 else slice(m * DH, m * DH + DH)
                        q = slice(tt * P, tt * P + P)
                        if tt == 0 and m == 0:
                            pe.wait_ge(z("qk_lo"), 2 * h + 2)
                            if kind == "f":
                                pe.wait_ge(z("sel_ready"), h + 1)
                        if not (isinstance(h, int) and h == 0 and tt == 0):
                            pe.wait_ge(z("exped"), (8 * h + tt - 1) * maps + m + 1)
                        for c in range((n + HALF - 1) // HALF):
                            w = min(HALF, n - c * HALF)
                            out, k = bank(2 + 2 * m + c)[:, 0:w], slice(c * HALF, c * HALF + w)
                            pe.matmul(out, g("QH")[rows, q], g("KH")[rows, k], start=True, stop=False)
                            pe.matmul(out, g("QH")[rows, q], g("KL")[rows, k], start=False, stop=False)
                            if kind == "f":
                                pe.matmul(out, fox["selc"][:, :], CHL[:, k], start=False, stop=False)
                            if (c + 1) * HALF >= n:
                                pe.matmul(out[:, w - P:w], identb[:, :], maskb[:, :], start=False, stop=False)
                            mm = pe.matmul(out, g("QL")[rows, q], g("KH")[rows, k], start=False, stop=True)
                        mm.then_inc(z("scored"), 1)

                def turn(h, tt, r):
                    done = 14 * h + (rounds(tt) + r)
                    if r == 0:
                        pe.wait_ge(z("combined" if kind == "d" else "exped"), 8 * h + tt + 1)
                    pe.wait_ge(z("turn_lo"), done)
                    for j in range(4 * r, min(4 * r + 4, tt + 1)):
                        tr = pe.transpose(bank(6)[:, (j - 4 * r) * P:(j - 4 * r + 1) * P],
                                          g("e0")[:, tt % 2, j * P:j * P + P], ident[:, :])
                    tr.then_inc(z("turned"), 1)

                def turn_v(h):
                    for r in range(2):
                        if r == 0:
                            pe.wait_ge(z("raw_written"), 6 * h + 6)
                        if r or not (isinstance(h, int) and h == 0):
                            pe.wait_ge(z("turn_lo"), 14 * h + r)
                        for j in range(4):
                            tr = pe.transpose(bank(6)[:, j * P:j * P + P],
                                              g("rawv")[:, (4 * r + j) * P:(4 * r + j + 1) * P], ident[:, :])
                        tr.then_inc(z("turned"), 1)

                def values(h, tt):
                    pe.wait_ge(z("turn_lo"), 14 * h + rounds(tt + 1))
                    if not (isinstance(h, int) and h == 0 and tt == 0):
                        pe.wait_ge(z("o_written"), 8 * h + tt)
                    for j in range(tt + 1):
                        mm = split_product(bank(7)[:, 0:P], g("PTH")[:, j, :], g("PTL")[:, j, :], g("VH")[:, j, :],
                                           g("VL")[:, j, :], j == 0, j == tt)
                    mm.then_inc(z("pv_done"), 1)

                def turn_o(h, tt):
                    pe.wait_ge(z("o_scaled"), 8 * h + tt + 1)
                    pe.transpose(bank(7)[:, 2 * P:3 * P], g("ot")[:, :], ident[:, :]).then_inc(z("o_turned"), 1)

                def head(h, nxt):
                    turn_v(h)
                    if not (isinstance(h, int) and h == 0):
                        turn_o(h - 1, NT - 1)
                    m = 0
                    for tt in range(NT + 1):
                        a, b = (6, SHARE[tt]) if tt < NT else (4, 8)
                        a, b = m + a, m + b
                        if tt < NT:
                            scores(h, tt)
                        if tt:
                            turn(h, tt - 1, 0)
                        if nxt is not None:
                            proj(nxt, m, a)
                        if tt >= 2:
                            turn_o(h, tt - 2)
                        if tt > 4:
                            turn(h, tt - 1, 1)
                        if nxt is not None:
                            proj(nxt, a, b)
                        if tt:
                            values(h, tt - 1)
                        m += SHARE[tt]
                        if nxt is not None:
                            proj(nxt, b, m)

                proj(0, 0, 144)
                head(0, 1)
                with pe.Fori(1, heads - 1) as h:
                    head(h, h + 1)
                head(heads - 1, None)
                turn_o(heads - 1, NT - 1)

            def out_projection(b0, first_k):
                for m in range(KT):
                    b = b0 + m
                    if m >= 2:
                        pe.wait_ge(s["out_added"], first_k + m - 1)
                    for half in range(2):
                        pe.wait_ge(s["w_split"], b + 1)
                        for k in range(KT):
                            if m == 0 and half == 0:
                                pe.wait_ge(s["o_split"], first_k + k + 1)
                            cs, ts = slice(k * P, k * P + P), slice(half * HALF, half * HALF + HALF)
                            mm = split_product(bank(2 * (m % 2) + half), WH[:, b % RING, cs], WL[:, b % RING, cs],
                                               HNH[:, k, ts], HNL[:, k, ts], k == 0, k == KT - 1)
                        mm.then_inc(s["first_half"] if half == 0 else s["blocks_freed"], 1)

            def feed_forward(layer, b0, norm_n):
                def up(n, pos, off):
                    start = isinstance(n, int) and n == 0
                    for j in range(2):
                        tile = 2 * n + (2 * GROUPS * layer + j)
                        for part, read, bk in ((0, "gate_taps", 0), (1, "gated", 2)):
                            if not (start and j == 0 and layer == 0):
                                pe.wait_ge(s[read], tile)
                            for half in range(2):
                                project(pos + (2 * j + part), (b0 + off + 2 * j + part) % RING, half, bank(bk + half),
                                        first_norm=norm_n if start and j == part == half == 0 else None)

                def down(n, pos, off, par):
                    pe.wait_ge(s["w_split"], pos + 2)
                    pe.wait_ge(s["hid_lo"], 2 * n + (2 * GROUPS * layer + 2))
                    for m in range(KT):
                        g = 8 * n + (8 * GROUPS * layer + m)
                        pe.wait_ge(s["down_added"], g + 1)
                        for half in range(2):
                            for j in range(2):
                                slot = (b0 + off + j) % RING
                                cs, ts = slice(m * P, m * P + P), slice(half * HALF, half * HALF + HALF)
                                mm = split_product(bank(4 + 2 * (m % 2) + half), WH[:, slot, cs], WL[:, slot, cs],
                                                   ffn["HH"][:, 2 * par + j, ts], ffn["HL"][:, 2 * par + j, ts],
                                                   j == 0, j == 1)
                        if m < KT - 1:
                            mm.then_inc(s["down_ready"], 1)
                        else:
                            mm.then_inc(s["blocks_freed"], 2)

                up(0, b0, 0)
                with pe.Fori(0, (GROUPS - 1) // 2) as i:
                    for q in range(2):
                        up(2 * i + (1 + q), 12 * i + (b0 + 4 + 6 * q), 4 + 6 * q)
                        down(2 * i + q, 12 * i + (b0 + 8 + 6 * q), 8 + 6 * q, q)
                down(GROUPS - 1, b0 + 6 * GROUPS - 2, 6 * GROUPS - 2, (GROUPS - 1) % 2)

            attention("f", fox, 1, H_FOX, B_FOX, 0)
            stage_end(pe, 4)
            out_projection(B_EVOUT, 0)
            stage_end(pe, 5)
            norm(1)
            feed_forward(0, B_FFN0, 1)
            stage_end(pe, 6)
            norm(2)
            stage_end(pe, 7)
            attention("d", dif, 2, H_DIFF, B_DIFF, 0)
            stage_end(pe, 8)
            out_projection(B_ODOUT, 8)
            stage_end(pe, 9)
            norm(3)
            feed_forward(1, B_FFN1, 3)
            stage_end(pe, 10)
            norm(4)

        @block.scalar
        def _(act):
            link = Chain(act, s["act_chain"])
            exp_ln = "natural_log_exp_and_others"

            def norm(n):
                for k in range(KT):
                    if k >= 2:
                        act.wait_ge(s["sq_added"], 8 * n + k - 1)
                    act.activation(sqb[:, k % 2, :], X[:, k, :], ACT.Square).then_inc(s["sq_done"], 1)
                act.wait_ge(s["sum_ready"], n + 1)
                act.activation(rt[:, :], bank(6, 2), ACT.Sqrt, bias=epsc[:, :], scale=1.0 / D).then_inc(
                    s["root_ready"], 1)
                if n < 4:
                    for k in range(KT):
                        act.wait_ge(s["hn_scaled"], 8 * n + k + 1)
                        act.activation(HNH[:, k, :], sqb[:, k % 2, :], ACT.Copy, scale=col(C_NORM + KT * n + k)).then_inc(
                            s["hn_hi"], 1)
                else:
                    for k in range(KT):
                        act.wait_ge(s["out_scaled"], k + 1)
                        act.activation(X[:, k, :], X[:, k, :], ACT.Copy, scale=col(C_NORM + KT * n + k)).then_inc(
                            s["out_w"], 1)
                        act.wait_ge(s["out_w"], k + 1)
                        act.dma_start(t["out"][k * P:(k + 1) * P, :], X[:, k, :]).then_inc(s["out_sent"], 16)
                    act.wait_ge(s["out_sent"], 16 * KT)

            act.dma_start(cols[:, :], t["cols"]).then_inc(s["consts_in"], 16)
            act.wait_ge(s["consts_in"], 16)
            act.dma_start(X[:, :, :], t["xT"].rearrange("(k p) n -> p k n", p=P)).then_inc(s["x_in"], 16)
            act.dma_start(ident[:, :], t["ident"]).then_inc(s["x_in"], 16)
            act.dma_start(dn["SC"][:, 0:P], t["mask"]).then_inc(s["x_in"], 16)
            act.dma_start(dnp["rst"][:, :], t["rst"]).then_inc(s["x_in"], 16)
            act.wait_ge(s["x_in"], 64)
            act.wait_ge(s["small_consts"], 1)
            norm(0)

            act.wait_ge(s["blocks_freed"], 1)
            act.wait_ge(s["hn_ready"], 8)
            act.activation(dnp["lg"][:, :], bank(0, 2), ACT.Copy).then_inc(s["conv_taps"], 1)
            for n in range(1, 13):
                act.wait_ge(s["blocks_freed"], n + 1)
                if n >= 3:
                    act.wait_ge(s["dn_silu"], n - 2)
                act.activation(dnp["dn_conv"][:, n % 2, :], bank(2 * (n % 2), 2), ACT.Copy,
                               scale=col(C_DNCONV + 4 * (n - 1) + 3)).then_inc(s["conv_start"], 1)
                act.wait_ge(s["conv_taps"], n + 1)
                if n >= 3:
                    act.wait_ge(dn_stored[n % 2], 16 * ((n - 1) // 2))
                act.activation(dnp["dn_out"][:, n % 2, :], dnp["dn_conv"][:, n % 2, :], ACT.Silu).then_inc(s["dn_silu"], 1)
                act.wait_ge(s["dn_silu"], n)
                act.dma_start(t["qkv"][n - 1, :, :], dnp["dn_out"][:, n % 2, :]).then_inc(dn_stored[n % 2], 16)
            act.wait_ge(s["rows_y"], 1)
            link(act.activation(dnp["lg_a"][:, :], dnp["lg"][:, :], ACT.Abs))
            link(act.activation(dnp["lg_a"][:, :], dnp["lg_a"][:, :], ACT.Exp, scale=-1.0))
            act.activation(dnp["lg_a"][:, :], dnp["lg_a"][:, :], ACT.Ln, bias=ones[:, 0:1]).then_inc(s["rows_l"], 1)
            act.activation(small[:, 0:1], col(C_ROW + 2), ACT.Exp).then_inc(s["rows_l"], 1)
            act.wait_ge(s["rows_scan"], 2)
            for q in range(2):
                act.wait_ge(dn_stored[q], 16 * 6)
            act.dma_start(dn["SELG"][:, :, :], t["selg"]).then_inc(s["rows_in"], 16)
            act.dma_start(dn["LM"][:, :, :], t["lm"]).then_inc(s["rows_in"], 16)
            act.dma_start(dn["MI"][:, :], t["mi"]).then_inc(s["rows_in"], 16)
            act.wait_ge(s["rows_in"], 48)
            for r in range(2):
                act.wait_ge(s["rows_turned"], r + 1)
                act.activation(dn["TKN"][:, 4 * r:4 * r + 4, :].rearrange("p t c -> p (t c)"), bank(4), ACT.Copy,
                               scale=-1.0).then_inc(s["rows_kept"], 1)
            act.wait_ge(s["rows_kept"], 2)
            act.activation(dn["TE"][:, :, :].rearrange("p t c -> p (t c)"),
                           dn["TKN"][:, :, :].rearrange("p t c -> p (t c)"), ACT.Exp, scale=-1.0).then_inc(s["te_ready"], 1)
            act.wait_ge(s["rows_turned"], 3)
            act.activation(dn["GLB"][:, :, :].rearrange("p h c -> p (h c)"), bank(5)[:, 0:64], ACT.Exp).then_inc(
                s["te_ready"], 1)
            stage_end(act, 1)

            d = dn
            flat = lambda a: a[:, :, :].rearrange("p h c -> p (h c)")

            def load_tile(i):
                qkv = t["qkv"].rearrange("(a h) p n -> a p h n", a=3)
                for a, n in enumerate(("qs", "ks", "vs")):
                    act.dma_start(d[n][:, :, :], qkv[a, :, :, bass.ts(i, P)]).then_inc(s["dn_loaded"], 16)

            def token_tile(i, last):
                act.wait_ge(s["dn_turn1"], i + 1)
                act.activation(flat(d["u"]), bank(2), ACT.Square).then_inc(s["dn_square"], 1)
                act.activation(flat(d["wT"]), bank(3), ACT.Square).then_inc(s["dn_square"], 1)
                act.wait_ge(s["dn_ss"], i + 1)
                link(act.activation(small[:, 16:24], small[:, 8:16], ACT.Ln, bias=epsc[:, :]))
                act.activation(small[:, 16:24], small[:, 16:24], ACT.Exp, scale=-0.5).then_inc(s["dn_root"], 1)
                for n, (dst, bk) in enumerate(((d["knT"][:, :, :], 5), (d["kbqT"][:, :, 0, :], 6),
                                               (d["kbqT"][:, :, 1, :], 7), (d["qgT"][:, :, :], 2))):
                    act.wait_ge(s["dn_turn2"], 4 * i + n + 1)
                    act.activation(dst, bank(bk).rearrange("p (h c) -> p h c", h=4), ACT.Copy).then_inc(s["dn_evac2"], 1)
                act.wait_ge(s["dn_dec"], i + 1)
                act.activation(flat(d["dec"]), flat(d["dec"]), ACT.Exp).then_inc(s["dn_exp"], 1)
                for lv in range(1, LEVELS):
                    act.wait_ge(s["dn_y"], (LEVELS - 1) * i + lv)
                    act.activation(flat(d["sq"]), bank(7), ACT.Copy).then_inc(s["dn_yc"], 1)
                act.wait_ge(s["dn_uw"], 2 * i + 2)
                act.activation(flat(d["wT"]), bank(4), ACT.Copy).then_inc(s["dn_wc"], 1)
                if not last:
                    load_tile(i + 1)
                act.wait_ge(s["dn_o"], 2 * i + 2)
                act.activation(flat(d["sq"]), bank(7), ACT.Square).then_inc(s["dn_osq"], 1)
                act.wait_ge(s["dn_oss"], i + 1)
                link(act.activation(small[:, 28:32], small[:, 24:28], ACT.Ln, bias=epsc[:, :], scale=1.0 / P))
                act.activation(small[:, 28:32], small[:, 28:32], ACT.Exp, scale=-0.5).then_inc(s["dn_ort"], 1)
                act.wait_ge(s["dn_ot"], i + 1)
                act.activation(X[:, 0:4, bass.ts(i, P)], bank(5).rearrange("p (h c) -> p h c", h=4), ACT.Copy,
                               scale=col(C_DNW)).then_inc(s["dn_ow"], 1)

            load_tile(0)
            act.preload_act_table_set(exp_ln)
            with act.Fori(0, NT - 1) as i:
                link.enter(i, 2)
                token_tile(i, False)
            link.leave(NT - 1)
            token_tile(NT - 1, True)
            stage_end(act, 2)

            for n in range(H_DN):
                act.wait_ge(s["blocks_freed"], B_Z + n + 1)
                if n >= 2:
                    act.wait_ge(s["z_done"], n - 1)
                act.activation(zst["z_gate"][:, n % 2, :], bank(2 * (n % 2), 2), ACT.Silu).then_inc(s["z_silu"], 1)
            stage_end(act, 3)

            def attention(kind, buf, maps, heads, b0, half0, o_tile, links):
                z = lambda n: s[f"{kind}_{n}"]
                g = lambda n: buf[f"{kind}_{n}"]
                scale = DH ** -0.5 if kind == "d" else 1.0

                def evacuate(hp, j):
                    if j % 2 == 0:
                        act.wait_ge(s["first_half"], 3 * hp + (half0 + j // 2 + 1))
                    else:
                        act.wait_ge(s["blocks_freed"], 3 * hp + (b0 + j // 2 + 1))
                    dst = g(("rawq", "rawk", "rawv")[j // 2])[:, (j % 2) * HALF:(j % 2 + 1) * HALF]
                    act.activation(dst, bank(j % 2), ACT.Copy,
                                   scale=P ** -0.5 if kind == "f" and j < 2 else 1.0).then_inc(z("raw_written"), 1)
                    if kind == "d" and j in (1, 3):
                        if j == 3:
                            act.wait_ge(z("roped"), 2 * hp + 1)
                        act.wait_ge(z("raw_written"), 6 * hp + j + 1)
                        raw = g(("rawq", "rawk")[j // 2])
                        for a, b in ((0, 32), (32, 0), (64, 96), (96, 64)):
                            act.dma_start(buf["xs"][a:a + 32, :], raw[b:b + 32, :]).then_inc(
                                z("swapped_q" if j == 1 else "swapped_k"), 16)

                def qk_high(h, which):
                    name, raw = ("QH", "rawq") if which == 0 else ("KH", "rawk")
                    if which == 0:
                        act.wait_ge(z("raw_written"), 6 * h + 4)
                        if kind == "d":
                            act.wait_ge(z("roped"), 2 * h + 2)
                    act.activation(g(name)[:, :], g(raw)[:, :], ACT.Copy).then_inc(z("qk_hi"), 1)

                def o_root(h, tt):
                    if kind == "d":
                        act.wait_ge(z("pv_done"), 8 * h + tt + 1)
                        act.activation(buf["sqd"][:, :], bank(7)[:, 0:P], ACT.Square,
                                       accum_out=buf["dsc"][:, 0:1]).then_inc(z("squared"), 1)
                        act.wait_ge(z("ss_ready"), 8 * h + tt + 1)
                        link(act.activation(buf["dsc"][:, 2:3], buf["dsc"][:, 1:2], ACT.Ln))
                        act.activation(buf["dsc"][:, 2:3], buf["dsc"][:, 2:3], ACT.Exp, scale=-0.5).then_inc(
                            z("rootd"), 1)

                def o_write(h, tt):
                    act.wait_ge(z("o_turned"), 8 * h + tt + 1)
                    act.activation(X[:, o_tile + h, tt * P:(tt + 1) * P], bank(7)[:, 2 * P:3 * P], ACT.Copy,
                                   scale=small[:, 40:41] if kind == "d" else 1.0).then_inc(z("o_written"), 1)

                def turned_high(h, tt, r):
                    act.wait_ge(z("turned"), 14 * h + (rounds(tt) + r + 1))
                    if r == 0 and tt:
                        act.wait_ge(z("pv_done"), 8 * h + tt)
                    c = min(4, tt + 1 - 4 * r)
                    act.activation(g("PTH")[:, 4 * r:4 * r + c, :],
                                   bank(6)[:, 0:c * P].rearrange("p (j c) -> p j c", j=c), ACT.Copy).then_inc(
                        z("turn_hi"), 1)

                def exponent(h, tt, m):
                    n = P * (tt + 1)
                    if m == 0 and tt >= 2:
                        act.wait_ge(z("turned"), 14 * h + rounds(tt - 1))
                    act.wait_ge(z("max_ready"), (8 * h + tt) * maps + m + 1)
                    act.activation(g("e0")[:, tt % 2, 0:n] if m == 0 else buf["e1"][:, 0:n], bank(2 + 2 * m, 2)[:, 0:n],
                                   ACT.Exp, bias=g("nmax")[:, m:m + 1], scale=scale,
                                   accum_out=g("sums")[:, tt % 2, m:m + 1]).then_inc(z("exped"), 1)

                def head(h, nxt):
                    for r in range(2):
                        act.wait_ge(z("turned"), 14 * h + r + 1)
                        act.activation(g("VH")[:, 4 * r:4 * r + 4, :], bank(6).rearrange("p (j c) -> p j c", j=4),
                                       ACT.Copy).then_inc(z("turn_hi"), 1)
                    if not (isinstance(h, int) and h == 0):
                        o_root(h - 1, NT - 1)
                        o_write(h - 1, NT - 1)
                    act.wait_ge(z("qk_lo"), 2 * h + 2)
                    for tt in range(NT + 1):
                        if tt >= 2:
                            o_root(h, tt - 2)
                        if tt:
                            turned_high(h, tt - 1, 0)
                        if tt < NT:
                            exponent(h, tt, 0)
                        elif nxt is not None:
                            qk_high(nxt, 0)
                        if tt >= 2:
                            o_write(h, tt - 2)
                        if tt > 4:
                            turned_high(h, tt - 1, 1)
                        if tt < NT and maps == 2:
                            exponent(h, tt, 1)
                        if nxt is not None:
                            if tt == NT:
                                qk_high(nxt, 1)
                            for j in HALVES_DONE[tt]:
                                evacuate(nxt, j)

                for j in range(6):
                    evacuate(0, j)
                act.preload_act_table_set(exp_ln)
                qk_high(0, 0)
                qk_high(0, 1)
                head(0, 1)
                with act.Fori(1, heads - 1) as h:
                    link.enter(h, links, 1)
                    head(h, h + 1)
                link.leave(heads - 2)
                head(heads - 1, None)
                o_root(heads - 1, NT - 1)
                o_write(heads - 1, NT - 1)

            def out_projection(x_src, first):
                for k in range(KT):
                    act.activation(HNH[:, k, :], X[:, k, :], ACT.Copy).then_inc(s["o_hi"], 1)
                for m in range(KT):
                    if m >= 2:
                        act.wait_ge(s["out_added"], first + m - 1)
                    act.dma_start(ost["xt"][:, m % 2, :], x_src[m * P:(m + 1) * P, :]).then_inc(s["x_back"], 16)
                    act.wait_ge(s["x_back"], 16 * (first + m + 1))

            def feed_forward(layer, b0):
                def tile(n, j, pos, par):
                    g = 2 * n + (2 * GROUPS * layer + j)
                    act.wait_ge(s["blocks_freed"], pos + (2 * j + 1))
                    act.wait_ge(s["params_in"], n + (GROUPS * layer + 1))
                    if not (isinstance(n, int) and n == 0 and j == 0 and layer == 0):
                        act.wait_ge(s["gated"], g)
                    act.activation(cv[:, j, :], bank(0, 2), ACT.Identity, scale=ffn["fp"][:, j, 2:3],
                                   bias=ffn["fp"][:, j, 3:4]).then_inc(s["gate_mid"], 1)
                    act.wait_ge(s["gate_taps"], g + 1)
                    act.activation(cv[:, j, :], cv[:, j, :], ACT.Silu).then_inc(s["silu_done"], 1)
                    act.wait_ge(s["gated"], g + 1)
                    act.activation(ffn["HH"][:, 2 * par + j, :], ffn["hb"][:, :], ACT.Copy).then_inc(s["hid_hi"], 1)

                for j in range(2):
                    tile(0, j, b0, 0)
                with act.Fori(0, (GROUPS - 1) // 2) as i:
                    for q in range(2):
                        for j in range(2):
                            tile(2 * i + (1 + q), j, 12 * i + (b0 + 4 + 6 * q), (1 + q) % 2)

            act.dma_start(fox["SELC"][:, :, :], t["selc"]).then_inc(s["rows_in"], 16)
            attention("f", fox, 1, H_FOX, B_FOX, B_FOX, 4, 0)
            stage_end(act, 4)
            out_projection(t["xT"], 0)
            stage_end(act, 5)
            norm(1)
            feed_forward(0, B_FFN0)
            stage_end(act, 6)
            act.dma_start(t["spill"].rearrange("(k p) n -> p k n", p=P), X[:, :, :]).then_inc(s["spilled"], 16)
            norm(2)
            act.wait_ge(s["spilled"], 16)
            stage_end(act, 7)
            act.dma_start(dif["cosT"][:, :], t["cosT"]).then_inc(s["spilled"], 16)
            act.dma_start(dif["sinT"][:, :], t["sinT"]).then_inc(s["spilled"], 16)
            act.wait_ge(s["spilled"], 48)
            act.wait_ge(s["rows_scan"], 4)
            act.activation(small[:, 44:46], small[:, 42:44], ACT.Exp).then_inc(s["rows_l"], 1)
            attention("d", dif, 2, H_DIFF, B_DIFF, B_DIFF - FT, 0, NT)
            stage_end(act, 8)
            out_projection(t["spill"], 8)
            stage_end(act, 9)
            norm(3)
            feed_forward(1, B_FFN1)
            stage_end(act, 10)
            norm(4)

        @block.vector
        def _(dve):
            link = Chain(dve, s["dve_chain"])

            def norm(n):
                for k in range(KT):
                    dve.wait_ge(s["sq_done"], 8 * n + k + 1)
                    if k == 0:
                        op = dve.tensor_copy(acc[:, :], sqb[:, 0, :])
                    else:
                        op = dve.tensor_tensor(acc[:, :], acc[:, :], sqb[:, k % 2, :], ALU.add)
                    op.then_inc(s["sq_added"], 1)
                    dve.wait_ge(s["sq_added"], 8 * n + k + 1)
                dve.wait_ge(s["root_ready"], n + 1)
                link(dve.reciprocal(rt[:, :], rt[:, :]))
                if n < 4:
                    def scaled(k):
                        if k >= 2:
                            dve.wait_ge(s["hn_ready"], 8 * n + k - 1)
                        dve.tensor_tensor(sqb[:, k % 2, :], X[:, k, :], rt[:, :], ALU.mult).then_inc(s["hn_scaled"], 1)

                    scaled(0)
                    for k in range(KT):
                        if k + 1 < KT:
                            scaled(k + 1)
                        dve.wait_ge(s["hn_hi"], 8 * n + k + 1)
                        dve.scalar_tensor_tensor(out=HNL[:, k, :], in0=sqb[:, k % 2, :], scalar=col(C_NORM + KT * n + k),
                                                 in1=HNH[:, k, :], op0=ALU.mult, op1=ALU.subtract).then_inc(
                            s["hn_ready"], 1)
                else:
                    for k in range(KT):
                        dve.tensor_tensor(X[:, k, :], X[:, k, :], rt[:, :], ALU.mult).then_inc(s["out_scaled"], 1)

            link(dve.memset(ones[:, :], 1.0))
            link(dve.memset(epsc[:, :], EPS))
            link(dve.memset(small[:, :], 0.0))
            dve.memset(small[:, 1:2], 0.0).then_inc(s["down_added"], 2)
            dve.wait_ge(s["consts_in"], 16)
            dve.wait_ge(s["x_in"], 64)
            link(dve.tensor_copy(identb[:, :], ident[:, :]))
            dve.tensor_copy(maskb[:, :], dn["SC"][:, 0:P]).then_inc(s["small_consts"], 1)
            norm(0)

            for n in range(1, 13):
                dve.wait_ge(s["conv_start"], n)
                buf, src = dnp["dn_conv"][:, n % 2, :], bank(2 * (n % 2), 2)
                for back in range(1, 4):
                    op = dve.scalar_tensor_tensor(out=buf[:, back:S], in0=src[:, 0:S - back],
                                                  scalar=col(C_DNCONV + 4 * (n - 1) + 3 - back), in1=buf[:, back:S],
                                                  op0=ALU.mult, op1=ALU.add)
                    if back < 3:
                        link(op)
                    else:
                        op.then_inc(s["conv_taps"], 1)
            dve.wait_ge(s["conv_taps"], 13)
            lg, la, lb = dnp["lg"], dnp["lg_a"], dnp["lg_b"]
            dve.tensor_scalar(lg[:, :], lg[:, :], col(C_ROW + 1), col(C_ROW), ALU.add, ALU.mult).then_inc(s["rows_y"], 1)
            dve.wait_ge(s["rows_l"], 2)
            link(dve.scalar_tensor_tensor(out=lb[:, :], in0=lg[:, :], scalar=0.0, in1=la[:, :], op0=ALU.max, op1=ALU.add))
            link(dve.tensor_scalar(lb[:, :], lb[:, :], small[:, 0:1], -1.0, ALU.mult, ALU.mult))
            SC = dn["SC"]
            dve.tensor_tensor_scan(lg[:, :], dnp["rst"][:, :], lb[:, :], 0.0, ALU.mult, ALU.add).then_inc(s["rows_scan"], 1)
            dve.wait_ge(s["rows_scan"], 1)
            link(dve.tensor_copy(la[:, :], lg[:, :]))
            g_rows = la[R_G:R_G + 32, :].rearrange("p (n c) -> p n c", c=CHUNK)
            link(dve.tensor_tensor(
                la[R_TAIL:R_TAIL + 32, :].rearrange("p (n c) -> p n c", c=CHUNK),
                g_rows[:, :, CHUNK - 1:CHUNK].to_broadcast([32, S // CHUNK, CHUNK]), g_rows, ALU.subtract))
            link(dve.memset(CHL[:, :].bitcast(F32), 0.0))
            link(dve.tensor_copy(CHL[R_F:R_F + 4, :], lg[R_F:R_F + 4, :]))
            link(dve.tensor_tensor(lb[R_F:R_F + 4, :], lg[R_F:R_F + 4, :], CHL[R_F:R_F + 4, :], ALU.subtract))
            link(dve.tensor_copy(CHL[R_TAIL:R_TAIL + 4, :], lb[R_F:R_F + 4, :]))
            dve.wait_ge(s["dn_silu"], 12)
            dve.tensor_copy(SC[:, :], la[:, :]).then_inc(s["rows_scan"], 1)
            dve.wait_ge(s["te_ready"], 2)
            for h in range(4):
                dve.memset(dn["St"][:, h, :], 0.0).then_inc(s["dn_sc"], 1)
            dve.wait_ge(s["dn_sc"], 4)
            stage_end(dve, 1)

            d = dn
            b4 = lambda a: bank(a).rearrange("p (h c) -> p h c", h=4)
            wide = lambda c: c.unsqueeze(2).to_broadcast([P, 4, P])
            with dve.Fori(0, NT) as i:
                link.enter(i, 23)
                link(dve.tensor_copy(d["te"][:, :], d["TE"][:, i, :]))
                link(dve.tensor_copy(d["tkn"][:, :], d["TKN"][:, i, :]))
                link(dve.tensor_copy(d["glt"][:, :, :], d["GLB"][:, :, bass.ts(i, 2)]))
                beta, eg, tail = (d["te"][:, r:r + 4] for r in (R_BETA, R_G, R_TAIL))
                dve.wait_ge(s["dn_square"], 2 * i + 2)
                link(dve.tensor_reduce(small[:, 8:12], d["u"][:, :, :], AX.X, ALU.add))
                dve.tensor_reduce(small[:, 12:16], d["wT"][:, :, :], AX.X, ALU.add).then_inc(s["dn_ss"], 1)
                dve.wait_ge(s["dn_root"], i + 1)

                def newton(y, x, tmp, add, mul):
                    link(dve.tensor_scalar(tmp, x, mul, add, ALU.mult, ALU.add))
                    link(dve.tensor_tensor(tmp, tmp, y, ALU.mult))
                    link(dve.tensor_tensor(tmp, tmp, y, ALU.mult))
                    link(dve.tensor_scalar(tmp, tmp, -0.5, 1.5, ALU.mult, ALU.add))
                    link(dve.tensor_tensor(y, y, tmp, ALU.mult))

                newton(small[:, 16:24], small[:, 8:16], small[:, 32:40], EPS, 1.0)
                rk, rq = small[:, 16:20], small[:, 20:24]
                fb, fbg, fd, fg = (small[:, c:c + 4] for c in (48, 52, 56, 60))
                link(dve.tensor_scalar(rq, rq, P ** -0.5, None, ALU.mult))
                link(dve.tensor_tensor(fb, rk, beta, ALU.mult))
                link(dve.tensor_tensor(fbg, fb, eg, ALU.mult))
                link(dve.tensor_tensor(fd, rk, tail, ALU.mult))
                link(dve.tensor_tensor(fg, rq, eg, ALU.mult))
                for n, bk, f in (("kn", 2, rk), ("kb", 2, fb), ("qn", 3, rq), ("qg", 3, fg), ("kbg", 2, fbg),
                                 ("kd", 2, fd), ("vb", 4, beta)):
                    dve.tensor_tensor(d[n][:, :, :], b4(bk), wide(f), ALU.mult).then_inc(s["dn_scale"], 1)
                dve.wait_ge(s["dn_pair"], 2 * i + 2)
                link(dve.tensor_tensor(d["dec"][:, :, :], b4(5), wide(d["tkn"][:, R_G:R_G + 4]), ALU.add))
                dve.tensor_scalar(d["dec"][:, :, :], d["dec"][:, :, :], 0.0, None, ALU.min).then_inc(s["dn_dec"], 1)
                dve.wait_ge(s["dn_exp"], i + 1)
                link(dve.tensor_tensor(d["dec"][:, :, :], d["dec"][:, :, :],
                                       d["MI"][:, :].unsqueeze(1).to_broadcast([P, 4, P]), ALU.mult))
                pair = bank(3, 2).rearrange("p (h a c) -> p h a c", h=4, a=2)
                link(dve.tensor_tensor(d["LT"][:, :, :], pair[:, :, 0, :], d["dec"][:, :, :], ALU.mult))
                dve.tensor_tensor(d["QKT"][:, :, :], pair[:, :, 1, :], d["dec"][:, :, :], ALU.mult).then_inc(
                    s["dn_mask"], 2)

                def level(lv):
                    dst = d["kn"] if lv == 0 else d[["kn", "kb"][lv % 2]]
                    return dve.tensor_tensor(dst[:, :, :], d["LT"][:, :, :],
                                             d["LM"][:, lv, :].unsqueeze(1).to_broadcast([P, 4, P]), ALU.mult)

                id4 = ident[:, :].unsqueeze(1).to_broadcast([P, 4, P])
                level(0).then_inc(s["dn_lts"], 1)
                level(1).then_inc(s["dn_lts"], 1)
                dve.wait_ge(s["dn_lts"], LEVELS * i + 1)
                dve.tensor_tensor(d["vs"][:, :, :], d["kn"][:, :, :], id4, ALU.add).then_inc(s["dn_xc"], 1)
                dve.wait_ge(s["dn_x1t"], i + 1)
                dve.tensor_tensor(d["qs"][:, :, :], b4(6), id4, ALU.add).then_inc(s["dn_xc"], 1)
                for lv in range(1, LEVELS):
                    dve.wait_ge(s["dn_xc"], 11 * i + 2 * lv)
                    if lv + 1 < LEVELS:
                        level(lv + 1).then_inc(s["dn_lts"], 1)
                    dve.wait_ge(s["dn_p"], 9 * i + (2 * lv - 1 if lv == LEVELS - 1 else 2 * lv))
                    dve.tensor_tensor(d["vs"][:, :, :], d["vs"][:, :, :], b4(2), ALU.add).then_inc(s["dn_xc"], 1)
                    if lv < LEVELS - 1:
                        dve.tensor_tensor(d["qs"][:, :, :], d["qs"][:, :, :], b4(5), ALU.add).then_inc(s["dn_xc"], 1)
                dve.wait_ge(s["dn_uw"], 2 * i + 1)
                link(dve.tensor_copy(d["u"][:, :, :], b4(3)))
                for c in range(2):
                    r = slice(c * CHUNK, c * CHUNK + CHUNK)
                    dve.wait_ge(s["dn_ws"], 2 * i + c + 1)
                    dve.tensor_tensor(d["vn"][r, :, :], d["u"][r, :, :], b4(6)[r, :, :], ALU.subtract).then_inc(
                        s["dn_vn"], 1)
                    dve.wait_ge(s["dn_s"], 2 * i + c + 1)
                    for h in range(4):
                        dve.scalar_tensor_tensor(out=d["St"][:, h, :], in0=d["St"][:, h, :], scalar=d["glt"][:, h, c:c + 1],
                                                 in1=b4(2)[:, h, :], op0=ALU.mult, op1=ALU.add).then_inc(s["dn_sc"], 1)
                    dve.wait_ge(s["dn_sc"], 8 * i + 8 + 4 * c)
                dve.wait_ge(s["dn_osq"], i + 1)
                dve.tensor_reduce(small[:, 24:28], d["sq"][:, :, :], AX.X, ALU.add).then_inc(s["dn_oss"], 1)
                dve.wait_ge(s["dn_ort"], i + 1)
                newton(small[:, 28:32], small[:, 24:28], small[:, 32:36], EPS, 1.0 / P)
                dve.tensor_tensor(d["on"][:, :, :], b4(7), wide(small[:, 28:32]), ALU.mult).then_inc(s["dn_on"], 1)
            link.leave(NT)
            stage_end(dve, 2)

            for n in range(H_DN):
                dve.wait_ge(s["z_silu"], n + 1)
                dve.tensor_tensor(X[:, n, :], X[:, n, :], zst["z_gate"][:, n % 2, :], ALU.mult).then_inc(s["z_done"], 1)
            stage_end(dve, 3)

            def attention(kind, buf, maps, heads, links):
                z = lambda n: s[f"{kind}_{n}"]
                g = lambda n: buf[f"{kind}_{n}"]

                def rope(hp, which):
                    raw, name = (g("rawq"), "swapped_q") if which == 0 else (g("rawk"), "swapped_k")
                    dve.wait_ge(z(name), 64 * hp + 64)
                    link(dve.tensor_tensor(buf["xs"][:, :], buf["xs"][:, :], buf["sinT"][:, :], ALU.mult))
                    link(dve.tensor_tensor(raw[:, :], raw[:, :], buf["cosT"][:, :], ALU.mult))
                    dve.tensor_tensor(raw[:, :], raw[:, :], buf["xs"][:, :], ALU.add).then_inc(z("roped"), 1)

                def qk_low(h, which):
                    hi, lo, raw = (("QH", "QL", "rawq"), ("KH", "KL", "rawk"))[which]
                    dve.wait_ge(z("qk_hi"), 2 * h + which + 1)
                    dve.tensor_tensor(g(lo)[:, :], g(raw)[:, :], g(hi)[:, :], ALU.subtract).then_inc(z("qk_lo"), 1)

                def o_sum(h, tt):
                    if kind == "d":
                        dve.wait_ge(z("squared"), 8 * h + tt + 1)
                        ss, x, ri = buf["dsc"][:, 0:1], buf["dsc"][:, 1:2], g("rinv")[:, tt % 4:tt % 4 + 1]
                        link(dve.tensor_scalar(x, ss, ri, ri, ALU.mult, ALU.mult))
                        dve.tensor_scalar(x, x, 1.0 / P, EPS, ALU.mult, ALU.add).then_inc(z("ss_ready"), 1)

                def o_scale(h, tt):
                    ri = g("rinv")[:, tt % 4:tt % 4 + 1]
                    if kind == "d":
                        x, y, w = buf["dsc"][:, 1:2], buf["dsc"][:, 2:3], buf["dsc"][:, 3:4]
                        dve.wait_ge(z("rootd"), 8 * h + tt + 1)
                        link(dve.tensor_scalar(w, y, y, x, ALU.mult, ALU.mult))
                        link(dve.tensor_scalar(w, w, -0.5, 1.5, ALU.mult, ALU.add))
                        link(dve.tensor_scalar(w, w, y, ri, ALU.mult, ALU.mult))
                        f = w
                    else:
                        dve.wait_ge(z("pv_done"), 8 * h + tt + 1)
                        f = ri
                    if tt or not (isinstance(h, int) and h == 0):
                        dve.wait_ge(z("o_turned"), 8 * h + tt)
                    dve.tensor_scalar(g("ot")[:, :], bank(7)[:, 0:P], f, None, ALU.mult).then_inc(z("o_scaled"), 1)

                def maximum(h, tt, m):
                    dve.wait_ge(z("scored"), (8 * h + tt) * maps + m + 1)
                    nm = g("nmax")[:, m:m + 1]
                    op = dve.tensor_reduce(nm, bank(2 + 2 * m, 2)[:, 0:P * (tt + 1)], AX.X, ALU.max, negate=True)
                    if kind == "d":
                        link(op)
                        op = dve.tensor_scalar(nm, nm, DH ** -0.5, None, ALU.mult)
                    op.then_inc(z("max_ready"), 1)

                def turned_low(h, tt, r):
                    dve.wait_ge(z("turn_hi"), 14 * h + (rounds(tt) + r + 1))
                    c = min(4, tt + 1 - 4 * r)
                    dve.tensor_tensor(g("PTL")[:, 4 * r:4 * r + c, :],
                                      bank(6)[:, 0:c * P].rearrange("p (j c) -> p j c", j=c),
                                      g("PTH")[:, 4 * r:4 * r + c, :], ALU.subtract).then_inc(z("turn_lo"), 1)

                def combine(h, tt):
                    n = P * (tt + 1)
                    dve.wait_ge(z("exped"), (8 * h + tt + 1) * maps)
                    su = lambda m: g("sums")[:, tt % 2, m:m + 1]
                    link(dve.reciprocal(g("rinv")[:, tt % 4:tt % 4 + 1], su(0)))
                    if kind == "d":
                        w = buf["dsc"][:, 4:5]
                        link(dve.reciprocal(w, su(1)))
                        link(dve.tensor_scalar(w, w, su(0), small[:, 41:42], ALU.mult, ALU.mult))
                        dve.scalar_tensor_tensor(out=g("e0")[:, tt % 2, 0:n], in0=buf["e1"][:, 0:n], scalar=w,
                                                 in1=g("e0")[:, tt % 2, 0:n], op0=ALU.mult, op1=ALU.add).then_inc(
                            z("combined"), 1)

                def head(h, nxt):
                    if kind == "f":
                        dve.tensor_copy(buf["selc"][:, :], buf["SELC"][:, h, :]).then_inc(z("sel_ready"), 1)
                    for r in range(2):
                        dve.wait_ge(z("turn_hi"), 14 * h + r + 1)
                        dve.tensor_tensor(g("VL")[:, 4 * r:4 * r + 4, :], bank(6).rearrange("p (j c) -> p j c", j=4),
                                          g("VH")[:, 4 * r:4 * r + 4, :], ALU.subtract).then_inc(z("turn_lo"), 1)
                    if not (isinstance(h, int) and h == 0):
                        o_sum(h - 1, NT - 1)
                        o_scale(h - 1, NT - 1)
                    for tt in range(NT + 1):
                        if tt >= 2:
                            o_sum(h, tt - 2)
                        if tt < NT:
                            maximum(h, tt, 0)
                        if tt >= 2:
                            o_scale(h, tt - 2)
                        if tt:
                            turned_low(h, tt - 1, 0)
                        if tt == NT and nxt is not None:
                            qk_low(nxt, 0)
                        if tt < NT and maps == 2:
                            maximum(h, tt, 1)
                        if tt > 4:
                            turned_low(h, tt - 1, 1)
                        if tt < NT:
                            combine(h, tt)
                        elif nxt is not None:
                            qk_low(nxt, 1)
                        if kind == "d" and nxt is not None and tt == 4:
                            rope(nxt, 0)
                        if kind == "d" and nxt is not None and tt == 7:
                            rope(nxt, 1)

                if kind == "d":
                    rope(0, 0)
                    rope(0, 1)
                qk_low(0, 0)
                qk_low(0, 1)
                head(0, 1)
                with dve.Fori(1, heads - 1) as h:
                    link.enter(h, links, 1)
                    head(h, h + 1)
                link.leave(heads - 2)
                head(heads - 1, None)
                o_sum(heads - 1, NT - 1)
                o_scale(heads - 1, NT - 1)

            def out_projection(b0, first):
                for k in range(KT):
                    dve.wait_ge(s["o_hi"], first + k + 1)
                    dve.tensor_tensor(HNL[:, k, :], X[:, k, :], HNH[:, k, :], ALU.subtract).then_inc(s["o_split"], 1)
                dve.wait_ge(s["o_split"], first + KT)
                for m in range(KT):
                    dve.wait_ge(s["blocks_freed"], b0 + m + 1)
                    dve.wait_ge(s["x_back"], 16 * (first + m + 1))
                    dve.tensor_tensor(X[:, m, :], bank(2 * (m % 2), 2), ost["xt"][:, m % 2, :], ALU.add).then_inc(
                        s["out_added"], 1)

            def feed_forward(layer, b0, links):
                def params(n):
                    at = C_FFN + layer * FT * 4
                    if isinstance(n, int):
                        src = cols[:, at + 8 * n:at + 8 * n + 8]
                    else:
                        src = cols[:, bass.ds(n * 8 + at, 8)]
                    dve.tensor_copy(ffn["fp"][:, :, :].rearrange("p a b -> p (a b)"), src).then_inc(s["params_in"], 1)

                def tile(n, j, pos, par):
                    g = 2 * n + (2 * GROUPS * layer + j)
                    dve.wait_ge(s["gate_mid"], g + 1)
                    c, ga = cv[:, j, :], bank(0, 2)
                    for back in (1, 2):
                        op = dve.scalar_tensor_tensor(out=c[:, back:S], in0=ga[:, 0:S - back],
                                                      scalar=ffn["fp"][:, j, 2 - back:3 - back], in1=c[:, back:S],
                                                      op0=ALU.mult, op1=ALU.add)
                        if back == 1:
                            link(op)
                        else:
                            op.then_inc(s["gate_taps"], 1)
                    dve.wait_ge(s["silu_done"], g + 1)
                    dve.wait_ge(s["blocks_freed"], pos + (2 * j + 2))
                    dve.tensor_tensor(ffn["hb"][:, :], bank(2, 2), c, ALU.mult).then_inc(s["gated"], 1)
                    dve.wait_ge(s["hid_hi"], g + 1)
                    dve.tensor_tensor(ffn["HL"][:, 2 * par + j, :], ffn["hb"][:, :], ffn["HH"][:, 2 * par + j, :],
                                      ALU.subtract).then_inc(s["hid_lo"], 1)

                def add_down(n, pos):
                    for m in range(KT):
                        g = 8 * n + (8 * GROUPS * layer + m)
                        if m < KT - 1:
                            dve.wait_ge(s["down_ready"], 7 * n + (7 * GROUPS * layer + m + 1))
                        else:
                            dve.wait_ge(s["blocks_freed"], pos + 2)
                        dve.tensor_tensor(X[:, m, :], X[:, m, :], bank(4 + 2 * (m % 2), 2), ALU.add).then_inc(
                            s["down_added"], 1)

                params(0)
                for j in range(2):
                    tile(0, j, b0, 0)
                with dve.Fori(0, (GROUPS - 1) // 2) as i:
                    link.enter(i, links)
                    for q in range(2):
                        params(2 * i + (1 + q))
                        for j in range(2):
                            tile(2 * i + (1 + q), j, 12 * i + (b0 + 4 + 6 * q), (1 + q) % 2)
                        add_down(2 * i + q, 12 * i + (b0 + 8 + 6 * q))
                link.leave((GROUPS - 1) // 2)
                add_down(GROUPS - 1, b0 + 6 * GROUPS - 2)

            dve.wait_ge(s["rows_in"], 64)
            attention("f", fox, 1, H_FOX, NT)
            stage_end(dve, 4)
            out_projection(B_EVOUT, 0)
            stage_end(dve, 5)
            norm(1)
            feed_forward(0, B_FFN0, 4)
            stage_end(dve, 6)
            norm(2)
            stage_end(dve, 7)
            dve.wait_ge(s["spilled"], 48)
            lam = lambda n: col(C_LAM + n * DH, DH)
            e = dif["xs"]
            link(dve.tensor_tensor(e[:, 0:DH], lam(0), lam(1), ALU.mult))
            link(dve.tensor_tensor(e[:, DH:2 * DH], lam(2), lam(3), ALU.mult))
            dve.tensor_reduce(small[:, 42:44], e[:, 0:2 * DH].rearrange("p (a b) -> p a b", a=2), AX.X, ALU.add).then_inc(
                s["rows_scan"], 1)
            dve.tensor_scalar(small[:, 40:41], col(C_SUBLN), 1.0 - LAMBDA_INIT, None, ALU.mult).then_inc(s["rows_scan"], 1)
            dve.wait_ge(s["rows_l"], 3)
            link(dve.tensor_tensor(small[:, 41:42], small[:, 45:46], small[:, 44:45], ALU.subtract))
            link(dve.tensor_scalar(small[:, 41:42], small[:, 41:42], -LAMBDA_INIT, None, ALU.add))
            attention("d", dif, 2, H_DIFF, 76)
            stage_end(dve, 8)
            out_projection(B_ODOUT, 8)
            stage_end(dve, 9)
            norm(3)
            feed_forward(1, B_FFN1, 4)
            stage_end(dve, 10)
            norm(4)


def _constants():
    k, c = np.arange(P)[:, None], np.arange(P)[None, :]
    same = k // CHUNK == c // CHUNK
    out = {"ident": np.eye(P), "mask": np.where(c <= k, 0.0, NEG)}
    out["mi"] = np.where(same & (k <= c), 1.0, 0.0)
    out["lm"] = np.stack([np.where((k // (2 << v) == c // (2 << v)) & ((k >> v) % 2 == 0) & ((c >> v) % 2 == 1), -1.0, 0.0)
                          for v in range(LEVELS)], axis=1)
    rst = np.zeros((P, S))
    rst[R_G:R_F] = (np.arange(S) % CHUNK != 0)
    rst[R_F:] = 1.0
    out["rst"] = rst
    selg, selc = np.zeros((P, 4, P)), np.zeros((P, 4, P))
    for h in range(4):
        selg[R_G + h, h] = 1.0
        selc[R_F + h, h] = -1.0
        selc[R_TAIL + h, h] = -1.0
    out["selg"], out["selc"] = selg, selc
    half = DH // 2
    inv = (1.0 / (10000.0 ** (np.arange(half, dtype=np.float32) * 2.0 / DH))).astype(np.float32)
    ang = inv[:, None] * np.arange(S, dtype=np.float32)[None, :]
    out["cosT"] = np.tile(np.cos(ang), (4, 1))
    out["sinT"] = np.concatenate([-np.sin(ang), np.sin(ang)] * 2)
    return {n: np.ascontiguousarray(a, dtype=np.float32) for n, a in out.items()}


def _column_blocks(w):
    n = w.shape[1] // P
    return w.reshape(KT, P, n, P).transpose(2, 1, 0, 3).reshape(n, P, D)


def _layout(a):
    w_in = a["ev_w_in"][0]
    at = np.cumsum([0, 3 * H_DN * P, H_DN * P, H_DN, H_DN, H_FOX * P, H_FOX * P, H_FOX * P, H_FOX])
    part = lambda n: w_in[:, at[n]:at[n + 1]]
    logits = np.zeros((D, P), np.float32)
    for r, n in ((R_BETA, 2), (R_G, 3), (R_F, 7)):
        logits[:, r:r + 4] = part(n)
    per_head = lambda q, k, v: np.stack([q, k, v], axis=1).reshape(-1, P, D)
    blocks = [_column_blocks(logits), _column_blocks(part(0)), _column_blocks(part(1)),
              per_head(*(_column_blocks(part(n)) for n in (4, 5, 6))), _column_blocks(a["ev_w_out"][0])]

    def feed_forward(layer):
        gate, val = np.split(_column_blocks(a["ffn_w_up"][layer]), 2)
        down = a["ffn_w_down"][layer].reshape(FT, P, D)
        up = lambda n: [gate[2 * n], val[2 * n], gate[2 * n + 1], val[2 * n + 1]]
        order = up(0)
        for n in range(1, GROUPS):
            order += up(n) + [down[2 * n - 2], down[2 * n - 1]]
        return np.stack(order + [down[-2], down[-1]])

    blocks.append(feed_forward(0))
    blocks.append(per_head(*(np.split(_column_blocks(a["od_w_in"][0]), 3))))
    blocks.append(_column_blocks(a["od_w_out"][0]))
    blocks.append(feed_forward(1))
    w = np.concatenate(blocks)
    assert w.shape[0] == N_BLOCKS

    tiles = lambda v: v.reshape(-1, P).T
    cols = np.zeros((P, N_COLS), np.float32)
    for n, v in enumerate((a["ev_norm_w"][0], a["ffn_norm_w"][0], a["od_norm_w"][0], a["ffn_norm_w"][1],
                           a["final_norm_w"])):
        cols[:, C_NORM + KT * n:C_NORM + KT * (n + 1)] = tiles(v)
    cols[:, C_DNCONV:C_FFN] = a["dn_conv_w"][0].reshape(4, 12, P).transpose(2, 1, 0).reshape(P, 48)
    for layer in range(2):
        taps = np.concatenate([a["ffn_conv_w"][layer], a["ffn_conv_b"][layer][None]]).reshape(4, FT, P)
        cols[:, C_FFN + layer * FT * 4:C_FFN + (layer + 1) * FT * 4] = taps.transpose(2, 1, 0).reshape(P, FT * 4)
    cols[:, C_DNW] = a["dn_norm_w"][0]
    cols[:, C_SUBLN] = a["diff_subln_w"][0]
    cols[:, C_LAM:C_ROW] = a["diff_lambda"][0].reshape(1, 4 * DH)
    cols[:, C_ROW] = 0.0
    for r, sign, bias, alog in ((R_BETA, -1.0, None, None), (R_G, 1.0, a["dn_dt_bias"][0], a["dn_a_log"][0]),
                                (R_F, -1.0, a["fox_f_bias"][0], None)):
        cols[r:r + 4, C_ROW] = sign
        if bias is not None:
            cols[r:r + 4, C_ROW + 1] = bias
        if alog is not None:
            cols[r:r + 4, C_ROW + 2] = alog
    return {"w": w, "cols": cols, "xT": np.ascontiguousarray(a["x"][0].T), **_constants()}


def kernel(**inputs):
    import concourse.bacc as _bacc
    from concourse.bass_utils import run_bass_kernel_spmd as _run

    arrays = _layout({n: np.asarray(v) for n, v in inputs.items()})
    nc = _bacc.Bacc("TRN2", target_bir_lowering=False, num_devices=1)
    t = {n: nc.dram_tensor(f"in_{n}", a.shape, mybir.dt.from_np(a.dtype), kind="ExternalInput").ap()
         for n, a in arrays.items()}
    t["out"] = nc.dram_tensor("out_T", [D, S], F32, kind="ExternalOutput").ap()
    t["qkv"] = nc.dram_tensor("qkv_scratch", [12, P, S], F32, kind="Internal").ap()
    t["spill"] = nc.dram_tensor("x_scratch", [D, S], F32, kind="Internal").ap()
    build(nc, t)
    r = _run(nc, [{f"in_{n}": a for n, a in arrays.items()}], core_ids=[0])
    return np.ascontiguousarray(r.results[0]["out_T"].T)[None]
```

```python
from contextlib import ExitStack

import numpy as np

import concourse.bass as bass
from concourse import mybir

F32, F32R, BF16 = mybir.dt.float32, mybir.dt.float32r, mybir.dt.bfloat16
ALU, ACT, AX = mybir.AluOpType, mybir.ActivationFunctionType, mybir.AxisListType

P = 128
D = 1024
S = 1024
KT = D // P
NT = S // P
HALF = 512
H_DN, H_FOX, H_DIFF = 4, 4, 8
DH = 64
CHUNK = 64
FF = 2816
FT = FF // P
GROUPS = FT // 2
EPS = 1e-6
NEG = -1e30
LAMBDA_INIT = 0.8 - 0.6 * float(np.exp(-0.3))

B_SMALL = 0
B_DN = 1
B_Z = B_DN + 3 * H_DN
B_FOX = B_Z + H_DN
B_EVOUT = B_FOX + 3 * H_FOX
B_FFN0 = B_EVOUT + KT
B_DIFF = B_FFN0 + 3 * FT
B_ODOUT = B_DIFF + 3 * H_DIFF
B_FFN1 = B_ODOUT + KT
N_BLOCKS = B_FFN1 + 3 * FT
RING = 3
assert N_BLOCKS % RING == 0

C_NORM = 0
C_DNCONV = C_NORM + 5 * KT
C_FFN = C_DNCONV + 12 * 4
C_DNW = C_FFN + 2 * FT * 4
C_SUBLN = C_DNW + 1
C_LAM = C_SUBLN + 1
C_ROW = C_LAM + 4 * DH
N_COLS = C_ROW + 3

R_BETA, R_G, R_F, R_TAIL = 0, 32, 64, 96
LEVELS = 6


SHARE = (25, 19, 16, 14, 13, 13, 13, 13, 18)
assert sum(SHARE) == 144
HALVES_DONE = [[j for j in range(6) if sum(SHARE[:n]) < 24 * (j + 1) <= sum(SHARE[:n + 1])] for n in range(9)]
assert all(len(x) < 2 for x in HALVES_DONE)
V_ROUNDS = (0, 2)
BESIDE = 3
PAUSES = dict(normed=26, turned=4, gated=4, paired=20, level_0=4,
              levels=((5, 7), (5, 7), (5, 7), (5, 7), (5, 5)), uw=4, state=((4, 6), (4, 10)))
assert (sum(n for n in PAUSES.values() if isinstance(n, int)) + sum(map(sum, PAUSES["levels"]))
        + sum(map(sum, PAUSES["state"]))) == 48 * BESIDE
KEPT = H_DN + 3 * H_FOX
assert (KEPT - 1) % BESIDE == 0
BUSY_TILES = (KEPT - 1) // BESIDE
rounds = lambda tile: 2 + tile + max(0, tile - 4) if tile else 1


class Chain:

    def __init__(self, engine, sem):
        self.engine, self.sem, self.start, self.n = engine, sem, 0, 0

    def __call__(self, instruction):
        instruction.then_inc(self.sem, 1)
        self.n += 1
        self.engine.wait_ge(self.sem, self.start + self.n)

    def enter(self, i, per, first=0):
        self.outer, self.per = self.start + self.n, per
        self.start, self.n = i * per + (self.outer - first * per), 0

    def leave(self, count):
        assert self.n == self.per, f"{self.engine}: {self.n} links in the body, not {self.per}"
        self.start, self.n = self.outer + count * self.per, 0


def build(nc, t, debug=None):
    with ExitStack() as ctx:
        sb = lambda name, shape, dt=F32: ctx.enter_context(nc.sbuf_tensor(name, shape, dt))

        X = sb("X", [P, KT, S])
        HNH = sb("HNH", [P, KT, S], F32R)
        HNL = sb("HNL", [P, KT, S], F32R)
        WRAW = sb("WRAW", [P, RING, D])
        WH = sb("WH", [P, RING, D], F32R)
        WL = sb("WL", [P, RING, D], F32R)
        ident = sb("ident", [P, P])
        ones = sb("ones", [P, P])
        cols = sb("cols", [P, N_COLS])
        epsc = sb("epsc", [P, 1])
        small = sb("small", [P, 64])
        tok = sb("tok", [P, 3 * NT])
        identb = sb("identb", [P, P], BF16)
        maskb = sb("maskb", [P, P], BF16)

        def stage(**shapes):
            with ExitStack() as own:
                return {n: own.enter_context(nc.sbuf_tensor(n, s, d)) for n, (s, d) in shapes.items()}

        even = ExitStack()
        CHL = even.enter_context(nc.sbuf_tensor("CHL", [P, S], F32R))
        PJ = even.enter_context(nc.sbuf_tensor("PJ", [P, 2, HALF], F32))
        row = ([P, S], F32)
        row_r = ([P, S], F32R)
        gates = ExitStack()
        gate = {n: gates.enter_context(nc.sbuf_tensor(n, s, F32)) for n, s in dict(
            SC=[P, S], TE=[P, NT, P], TKN=[P, NT, P], GLB=[P, 4, 16], SELG=[P, 4, P], LM=[P, LEVELS, P], MI=[P, P]).items()}
        dnp = stage(dn_conv=([P, 2, S], F32), dn_out=([P, 2, S], F32), lg=row, lg_a=row, lg_b=row, rst=row)
        four = ([P, 4, P], F32)
        dn = stage(
            te=([P, P], F32), tkn=([P, P], F32), glt=([P, 4, 2], F32),
            qs=four, ks=four, vs=four, sq=four, kn=four, kb=four, qn=four, qg=four, kbg=four, kd=four, vb=four,
            knT=four, kbqT=([P, 4, 2, P], F32), qgT=four, dec=four, QKT=four, LT=four, u=four, wT=four, vn=four,
            St=four,
        )
        dn.update(gate)
        gates.close()
        att = dict(
            rawq=row, rawk=row, rawv=row, QH=row_r, QL=row_r, KH=row_r, KL=row_r,
            VHL=([P, NT, 2, P], F32R), PTH=([P, NT, P], F32R), PTL=([P, NT, P], F32R),
            e0=([P, 2, S], F32), ot=([P, P], F32), sums=([P, 2, 2], F32), nmax=([P, 2], F32), rinv=([P, 4], F32),
        )
        fox = stage(**{f"f_{k}": v for k, v in att.items()}, SELC=([P, 4, P], F32), selc=([P, P], F32R))
        even.close()
        dif = stage(**{f"d_{k}": v for k, v in att.items()}, e1=row, xs=row, cosT=row, sinT=row,
                    dsc=([P, 8], F32))
        ost = stage(xt=([P, 2, S], F32))
        ffn = stage(
            HH=([P, 4, S], F32R), HL=([P, 4, S], F32R), cv=([P, 2, S], F32), hb=([P, S], F32), fp=([P, 2, 4], F32),
            sqb=([P, 2, S], F32), acc=row, rt=row,
        )
        sqb, acc, rt = ffn["sqb"], ffn["acc"], ffn["rt"]
        cv = ffn["cv"]

        ps = ctx.enter_context(nc.psum_tensor("ps", [P, 8, HALF], F32))
        bank = lambda b, n=1: ps[:, b:b + n, :].rearrange("p b c -> p (b c)")

        names = (
            "diagonal spread consts_in x_in rst_in spilled w_split w_split_hi blocks_freed first_half small_consts "
            "sq_done sq_added sum_ready root_ready hn_scaled hn_hi hn_ready out_scaled out_sent out_w "
            "kept_written z_in pe_chain pool_chain act_chain dve_chain stage_end "
            "conv_start conv_taps dn_silu rows_in rows_y rows_abs rows_l rows_scan rows_turned rows_kept "
            "rows_tail glb_ready te_ready chl_ready "
            "dn_loaded dn_staged dn_turn1 dn_square dn_ss dn_root dn_scale dn_turn2 dn_evac2 dn_pair dn_dec dn_exp dn_mask "
            "dn_x1t dn_x1 dn_lts dn_y dn_yc dn_p dn_xc dn_uw dn_uc dn_wc dn_ws dn_vn dn_o dn_s dn_sc dn_osq dn_oss "
            "dn_ort dn_on dn_ot dn_ow z_silu z_done "
            "o_hi o_split x_back xt_free out_added "
            "gate_mid gate_taps silu_done gated hid_hi hid_lo params_in down_ready down_added "
        ).split()
        sem = {n: ctx.enter_context(nc.semaphore(n)) for n in names}
        w_loaded = [ctx.enter_context(nc.semaphore(f"w_loaded{i}")) for i in range(RING)]
        kept_stored = [ctx.enter_context(nc.semaphore(f"kept_stored{i}")) for i in range(2)]
        x_part = [ctx.enter_context(nc.semaphore(f"x_part{i}")) for i in range(KT // 2)]
        dn_stored = [ctx.enter_context(nc.semaphore(f"dn_stored{i}")) for i in range(2)]
        for kind in "fd":
            for n in ("raw_written swapped_q swapped_k roped qk_hi qk_lo turned turn_hi turn_lo scored max_ready exped raw_in o_summed "
                      "combined pv_done squared ss_ready rootd o_scaled o_turned o_written sel_ready").split():
                sem[f"{kind}_{n}"] = ctx.enter_context(nc.semaphore(f"{kind}_{n}"))
        s = sem
        block = ctx.enter_context(nc.Block())

        col = lambda c, n=1: cols[:, c:c + n]

        @block.sync
        def _(sp):
            def load(b, place):
                sp.wait_ge(s["w_split"], b - RING + 1)
                sp.dma_start(WRAW[:, place % RING, :], t["w"][b, :, :]).then_inc(w_loaded[place % RING], 16)

            def load_run(b0, b1):
                turns = (b1 - b0) // RING
                with sp.Fori(0, turns) as i:
                    for j in range(RING):
                        load(i * RING + (b0 + j), b0 + j)
                for b in range(b0 + turns * RING, b1):
                    load(b, b)

            def swap_halves(h, which):
                sp.wait_ge(s["d_raw_written"], 6 * h + (2 + 2 * which))
                raw = dif[("d_rawq", "d_rawk")[which]]
                dst = dif["e1" if isinstance(h, int) and which == 0 else "xs"]
                for a, b in ((0, 32), (32, 0), (64, 96), (96, 64)):
                    sp.dma_start(dst[a:a + 32, :], raw[b:b + 32, :]).then_inc(
                        s[("d_swapped_q", "d_swapped_k")[which]], 16)

            def head_loads(h):
                for part in range(3):
                    if part != 1:
                        swap_halves(h, part // 2)
                    load(3 * h + (B_DIFF + 2 * RING + part), B_DIFF + part)

            for b in range(RING):
                sp.dma_start(WRAW[:, b, :], t["w"][b, :, :]).then_inc(w_loaded[b], 16)
            def keep(e):
                for half in range(2):
                    sp.wait_ge(s["kept_written"], 2 * e + (half + 1))
                    sp.dma_start(t["kept"][e, :, half * HALF:half * HALF + HALF], PJ[:, half, :]).then_inc(
                        kept_stored[half], 16)

            def fetch(h):
                for c, name in enumerate(("rawq", "rawk", "rawv")):
                    sp.dma_start(fox[f"f_{name}"][:, :], t["kept"][3 * h + (H_DN + c), :, :]).then_inc(s["f_raw_in"], 16)

            load_run(RING, B_Z + RING)
            load(B_Z + RING, B_Z + RING)
            keep(0)
            with sp.Fori(0, BUSY_TILES) as i:
                for j in range(BESIDE):
                    load(BESIDE * i + (B_Z + 1 + j + RING), B_Z + 1 + j + RING)
                    keep(BESIDE * i + (1 + j))
            for half in range(2):
                sp.wait_ge(kept_stored[half], 16 * KEPT)
            sp.dma_start(X[:, H_DN:2 * H_DN, :], t["kept"][0:H_DN, :, :].rearrange("e p n -> p e n")).then_inc(s["z_in"], 16)
            sp.wait_ge(s["stage_end"], 6)
            fetch(0)
            with sp.Fori(1, H_FOX) as h:
                sp.wait_ge(s["f_turned"], 14 * h - 11)
                fetch(h)
            load_run(B_EVOUT + RING, B_DIFF + 2 * RING)
            swap_halves(0, 0)
            swap_halves(0, 1)
            for part in range(3):
                load(B_DIFF + 2 * RING + part, B_DIFF + part)
            with sp.Fori(1, H_DIFF) as h:
                head_loads(h)
            load_run(B_DIFF + 3 * H_DIFF + 2 * RING, N_BLOCKS)
            for k in range(KT):
                sp.wait_ge(s["out_scaled"], k + 1)
                sp.dma_start(t["out"][k * P:(k + 1) * P, :], X[:, k, :]).then_inc(s["out_sent"], 16)
            sp.wait_ge(s["out_sent"], 16 * KT)

        @block.gpsimd
        def _(pool):
            def split(b, slot, turn):
                pool.wait_ge(w_loaded[slot], turn * 16 + 16)
                pool.tensor_tensor(WH[:, slot, :], WRAW[:, slot, :], ones[:, 0:1].to_broadcast([P, D]), ALU.mult).then_inc(
                    s["w_split_hi"], 1)
                pool.wait_ge(s["w_split_hi"], b + 1)
                pool.tensor_tensor(WL[:, slot, :], WRAW[:, slot, :], WH[:, slot, :], ALU.subtract).then_inc(
                    s["w_split"], 1)

            def split_next(b, place, turn):
                pool.wait_ge(s["blocks_freed"], b - RING + 1)
                split(b, place % RING, turn + place // RING)

            def split_run(b0, b1):
                rounds = (b1 - b0) // RING
                if rounds:
                    with pool.Fori(0, rounds) as i:
                        for j in range(RING):
                            split_next(i * RING + (b0 + j), b0 + j, i)
                for b in range(b0 + rounds * RING, b1):
                    split_next(b, b, 0)

            link = Chain(pool, s["pool_chain"])

            def rope(h, which):
                raw, name = (dif["d_rawq"], "swapped_q") if which == 0 else (dif["d_rawk"], "swapped_k")
                pool.wait_ge(s[f"d_{name}"], 64 * h + 64)
                link(pool.tensor_tensor(dif["xs"][:, :], dif["xs"][:, :], dif["sinT"][:, :], ALU.mult))
                link(pool.tensor_tensor(raw[:, :], raw[:, :], dif["cosT"][:, :], ALU.mult))
                pool.tensor_tensor(raw[:, :], raw[:, :], dif["xs"][:, :], ALU.add).then_inc(s["d_roped"], 1)

            def qk_low(h, which):
                hi, lo, raw = (("QH", "QL", "rawq"), ("KH", "KL", "rawk"))[which]
                pool.wait_ge(s["d_qk_hi"], 2 * h + which + 1)
                pool.tensor_tensor(dif[f"d_{lo}"][:, :], dif[f"d_{raw}"][:, :], dif[f"d_{hi}"][:, :],
                                   ALU.subtract).then_inc(s["d_qk_lo"], 1)

            pool.wait_ge(s["small_consts"], 1)
            for b in range(RING):
                split(b, b, 0)
            split_run(RING, B_DIFF + RING)
            for part in range(3):
                split_next(B_DIFF + 3 + part, B_DIFF + 3 + part, 0)
            with pool.Fori(1, H_DIFF) as h:
                link.enter(h, 4, 1)
                for part in range(3):
                    if part == 2:
                        qk_low(h, 0)
                        qk_low(h, 1)
                    split_next(3 * h + (B_DIFF + 3 + part), B_DIFF + 3 + part, h)
                    if part < 2:
                        rope(h, part)
            link.leave(H_DIFF - 1)
            split_run(B_DIFF + 3 * H_DIFF + 3, N_BLOCKS)

        def stage_end(eng, n, wait=True):
            eng.drain().then_inc(s["stage_end"], 1)
            if wait:
                eng.wait_ge(s["stage_end"], 3 * n)

        @block.tensor
        def _(pe):
            def split_product(out, wh, wl, xh, xl, first, last):
                pe.matmul(out, wh, xh, start=first, stop=False)
                pe.matmul(out, wh, xl, start=False, stop=False)
                return pe.matmul(out, wl, xh, start=False, stop=last)

            def project_arriving(n, b):
                for k in range(KT):
                    pe.wait_ge(s["hn_ready"], 8 * n + k + 1)
                    for j in range(2):
                        if k == 0:
                            pe.wait_ge(s["w_split"], b + j + 1)
                        slot, cs = (b + j) % RING, slice(k * P, k * P + P)
                        for half in range(2):
                            ts = slice(half * HALF, half * HALF + HALF)
                            mm = split_product(bank(2 * j + half), WH[:, slot, cs], WL[:, slot, cs], HNH[:, k, ts],
                                               HNL[:, k, ts], k == 0, k == KT - 1)
                            if k == KT - 1:
                                mm.then_inc(s["first_half"] if half == 0 else s["blocks_freed"], 1)

            def project(b, slot, half, out):
                if half == 0:
                    pe.wait_ge(s["w_split"], b + 1)
                for k in range(KT):
                    cs, ts = slice(k * P, k * P + P), slice(half * HALF, half * HALF + HALF)
                    mm = split_product(out, WH[:, slot, cs], WL[:, slot, cs], HNH[:, k, ts], HNL[:, k, ts],
                                       k == 0, k == KT - 1)
                mm.then_inc(s["first_half"] if half == 0 else s["blocks_freed"], 1)

            def norm(n):
                pe.wait_ge(s["sq_added"], 8 * n + 8)
                for tt in range(NT):
                    mm = pe.matmul(bank(6)[:, tt:tt + 1], acc[:, tt * P:tt * P + P], ones[:, 0:1], start=True, stop=True)
                mm.then_inc(s["sum_ready"], 1)
                pe.wait_ge(s["diagonal"], n + 1)
                for h in range(2):
                    mm = pe.matmul(bank(6 + h), ones[:, :], rt[:, h * HALF:h * HALF + HALF], start=True, stop=True)
                mm.then_inc(s["spread"], 1)

            pe.wait_ge(s["small_consts"], 1)
            pe.wait_ge(s["consts_in"], 16)
            norm(0)
            project_arriving(0, B_SMALL)
            for n in range(2, 14):
                b = B_SMALL + n
                if n >= 3:
                    pe.wait_ge(s["conv_taps"], n - 2)
                for half in range(2):
                    project(b, b % RING, half, bank(2 * (n % 3) + half))
                if n == 9:
                    pe.wait_ge(s["rows_scan"], 2)
                    for r in range(2):
                        for j in range(4):
                            tr = pe.transpose(bank(6 + r)[:, j * P:j * P + P], dn["SC"][:, (4 * r + j) * P:(4 * r + j + 1) * P],
                                              ident[:, :])
                        tr.then_inc(s["rows_turned"], 1)
                if n == 10:
                    pe.wait_ge(s["rows_in"], 48)
                    pe.wait_ge(s["rows_kept"], 1)
                    for h in range(4):
                        mm = pe.matmul(bank(6)[:, h * 16:h * 16 + 16], dn["SELG"][:, h, :],
                                       dn["SC"][:, CHUNK - 1:S:CHUNK], start=True, stop=True)
                    mm.then_inc(s["rows_turned"], 1)
            stage_end(pe, 1)

            d = dn

            def turn4(bk, src, name=None):
                for h in range(4):
                    tr = pe.transpose(bank(bk)[:, h * P:h * P + P], src[:, h, :], ident[:, :])
                return tr

            def beside(i, m0, n):
                for m in range(m0, m0 + n):
                    j, half, k, p = m // 48, m % 48 // 24, m % 24 // 3, m % 3
                    slot = (B_Z + 1 + j) % RING
                    if m % 48 == 0:
                        pe.wait_ge(s["w_split"], BESIDE * i + (B_Z + 2 + j))
                    if m % 24 == 0:
                        pe.wait_ge(s["kept_written"], 2 * BESIDE * i + (2 * j + half + 1))
                    cs, ts = slice(k * P, k * P + P), slice(half * HALF, half * HALF + HALF)
                    mm = pe.matmul(bank(half), (WL if p == 2 else WH)[:, slot, cs],
                                   (HNL if p == 1 else HNH)[:, k, ts], start=m % 24 == 0, stop=m % 24 == 23)
                    if m % 24 == 23:
                        mm.then_inc(s["first_half"] if half == 0 else s["blocks_freed"], 1)

            def token_tile(i, busy):
                at = 0

                def pause(n):
                    nonlocal at
                    if busy:
                        beside(i, at, n)
                    at += n

                pe.wait_ge(s["dn_loaded"], 48 * i + 48)
                pe.wait_ge(s["dn_sc"], 8 * i + 4)
                turn4(2, d["ks"])
                turn4(3, d["qs"])
                turn4(4, d["vs"]).then_inc(s["dn_turn1"], 1)
                pause(PAUSES["normed"])
                pe.wait_ge(s["dn_scale"], 7 * i + 2)
                turn4(5, d["kn"]).then_inc(s["dn_turn2"], 1)
                turn4(6, d["kb"]).then_inc(s["dn_turn2"], 1)
                pe.wait_ge(s["dn_scale"], 7 * i + 4)
                turn4(7, d["qn"]).then_inc(s["dn_turn2"], 1)
                pause(PAUSES["turned"])
                pe.wait_ge(s["dn_scale"], 7 * i + 7)
                turn4(2, d["qg"]).then_inc(s["dn_turn2"], 1)
                pause(PAUSES["gated"])
                pe.wait_ge(s["dn_evac2"], 4 * i + 4)
                for h in range(4):
                    mm = pe.matmul(bank(3 + h // 2)[:, (h % 2) * 2 * P:(h % 2 + 1) * 2 * P], d["knT"][:, h, :],
                                   d["kbqT"][:, h, :, :].rearrange("p a c -> p (a c)"), start=True, stop=True)
                mm.then_inc(s["dn_pair"], 1)
                for h in range(4):
                    mm = pe.matmul(bank(5)[:, h * P:h * P + P], d["SELG"][:, h, :], d["SC"][:, bass.ts(i, P)],
                                   start=True, stop=True)
                mm.then_inc(s["dn_pair"], 1)
                pause(PAUSES["paired"])
                pe.wait_ge(s["dn_lts"], LEVELS * i + 1)
                turn4(6, d["kn"]).then_inc(s["dn_x1t"], 1)
                pause(PAUSES["level_0"])
                for lv in range(1, LEVELS):
                    pe.wait_ge(s["dn_lts"], LEVELS * i + lv + 1)
                    pe.wait_ge(s["dn_xc"], 11 * i + 2 * lv)
                    for h in range(4):
                        mm = pe.matmul(bank(7)[:, h * P:h * P + P], d[["kn", "kb"][lv % 2]][:, h, :], d["qs"][:, h, :],
                                       start=True, stop=True)
                    mm.then_inc(s["dn_y"], 1)
                    pause(PAUSES["levels"][lv - 1][0])
                    pe.wait_ge(s["dn_yc"], (LEVELS - 1) * i + lv)
                    for h in range(4):
                        mm = pe.matmul(bank(2)[:, h * P:h * P + P], d["sq"][:, h, :], d["vs"][:, h, :],
                                       start=True, stop=True)
                    mm.then_inc(s["dn_p"], 1)
                    if lv < LEVELS - 1:
                        for h in range(4):
                            mm = pe.matmul(bank(5)[:, h * P:h * P + P], d["vs"][:, h, :], d["sq"][:, h, :],
                                           start=True, stop=True)
                        mm.then_inc(s["dn_p"], 1)
                    pause(PAUSES["levels"][lv - 1][1])
                pe.wait_ge(s["dn_xc"], 11 * i + 11)
                for h in range(4):
                    mm = pe.matmul(bank(3)[:, h * P:h * P + P], d["vs"][:, h, :], d["vb"][:, h, :], start=True, stop=True)
                mm.then_inc(s["dn_uw"], 1)
                for h in range(4):
                    mm = pe.matmul(bank(4)[:, h * P:h * P + P], d["kbg"][:, h, :], d["vs"][:, h, :], start=True, stop=True)
                mm.then_inc(s["dn_uw"], 1)
                pause(PAUSES["uw"])
                for c in range(2):
                    r = slice(c * CHUNK, c * CHUNK + CHUNK)
                    if c == 0:
                        pe.wait_ge(s["dn_wc"], i + 1)
                        pe.wait_ge(s["dn_sc"], 8 * i + 4)
                    else:
                        pe.wait_ge(s["dn_sc"], 8 * i + 8)
                    for h in range(4):
                        mm = pe.matmul(bank(6)[r, h * P:h * P + P], d["wT"][:, h, r], d["St"][:, h, :],
                                       start=True, stop=True)
                    mm.then_inc(s["dn_ws"], 1)
                    pause(PAUSES["state"][c][0])
                    if c == 0:
                        pe.wait_ge(s["dn_mask"], 2 * i + 2)
                    pe.wait_ge(s["dn_vn"], 2 * i + c + 1)
                    for h in range(4):
                        o = bank(7)[r, h * P:h * P + P]
                        pe.matmul(o, d["qgT"][:, h, r], d["St"][:, h, :], start=True, stop=False)
                        mm = pe.matmul(o, d["QKT"][r, h, r], d["vn"][r, h, :], start=False, stop=True)
                    mm.then_inc(s["dn_o"], 1)
                    for h in range(4):
                        mm = pe.matmul(bank(2)[:, h * P:h * P + P], d["kd"][r, h, :], d["vn"][r, h, :],
                                       start=True, stop=True)
                    mm.then_inc(s["dn_s"], 1)
                    pause(PAUSES["state"][c][1])
                pe.wait_ge(s["dn_on"], i + 1)
                turn4(5, d["dec"]).then_inc(s["dn_ot"], 1)

            with pe.Fori(0, BUSY_TILES) as i:
                token_tile(i, True)
            with pe.Fori(BUSY_TILES, NT) as i:
                token_tile(i, False)
            stage_end(pe, 2)

            stage_end(pe, 3)

            def attention(kind, buf, maps, heads, b0, halves_before):
                z = lambda n: s[f"{kind}_{n}"]
                g = lambda n: buf[f"{kind}_{n}"]

                def proj(hp, m0, m1):
                    for m in range(m0, m1):
                        j, k, p = m // 24, m % 24 // 3, m % 3
                        slot, half = (b0 + j // 2) % RING, j % 2
                        if m % 48 == 0:
                            pe.wait_ge(s["w_split"], 3 * hp + (b0 + j // 2 + 1))
                        if m % 24 == 0 and not (isinstance(hp, int) and hp == 0 and j < 2):
                            pe.wait_ge(z("raw_written"), 6 * hp + (j - 1))
                        cs, ts = slice(k * P, k * P + P), slice(half * HALF, half * HALF + HALF)
                        mm = pe.matmul(bank(half), (WL if p == 2 else WH)[:, slot, cs],
                                       (HNL if p == 1 else HNH)[:, k, ts], start=m % 24 == 0, stop=m % 24 == 23)
                        if m % 24 == 23:
                            mm.then_inc(s["first_half"] if half == 0 else s["blocks_freed"], 1)

                def scores(h, tt):
                    n = P * (tt + 1)
                    for m in range(maps):
                        rows = slice(0, P) if maps == 1 else slice(m * DH, m * DH + DH)
                        q = slice(tt * P, tt * P + P)
                        if tt == 0 and m == 0:
                            pe.wait_ge(z("qk_lo"), 2 * h + 2)
                            if kind == "f":
                                pe.wait_ge(z("sel_ready"), h + 1)
                        if not (isinstance(h, int) and h == 0 and tt == 0):
                            pe.wait_ge(z("exped"), (8 * h + tt - 1) * maps + m + 1)
                        for c in range((n + HALF - 1) // HALF):
                            w = min(HALF, n - c * HALF)
                            out, k = bank(2 + 2 * m + c)[:, 0:w], slice(c * HALF, c * HALF + w)
                            pe.matmul(out, g("QH")[rows, q], g("KH")[rows, k], start=True, stop=False)
                            pe.matmul(out, g("QH")[rows, q], g("KL")[rows, k], start=False, stop=False)
                            if kind == "f":
                                pe.matmul(out, fox["selc"][:, :], CHL[:, k], start=False, stop=False)
                            if (c + 1) * HALF >= n:
                                pe.matmul(out[:, w - P:w], identb[:, :], maskb[:, :], start=False, stop=False)
                            mm = pe.matmul(out, g("QL")[rows, q], g("KH")[rows, k], start=False, stop=True)
                        mm.then_inc(z("scored"), 1)

                def turn(h, tt, r):
                    done = 14 * h + (rounds(tt) + r)
                    if r == 0:
                        pe.wait_ge(z("combined" if kind == "d" else "exped"), 8 * h + tt + 1)
                    pe.wait_ge(z("turn_lo"), done)
                    for j in range(4 * r, min(4 * r + 4, tt + 1)):
                        tr = pe.transpose(bank(6)[:, (j - 4 * r) * P:(j - 4 * r + 1) * P],
                                          g("e0")[:, tt % 2, j * P:j * P + P], ident[:, :])
                    tr.then_inc(z("turned"), 1)

                def turn_v(h, r):
                    if r == 0:
                        if kind == "d":
                            pe.wait_ge(z("raw_written"), 6 * h + 6)
                        else:
                            pe.wait_ge(z("raw_in"), 48 * h + 48)
                    if r or not (isinstance(h, int) and h == 0):
                        pe.wait_ge(z("turn_lo"), 14 * h + V_ROUNDS[r])
                    for j in range(4):
                        tr = pe.transpose(bank(6)[:, j * P:j * P + P],
                                          g("rawv")[:, (4 * r + j) * P:(4 * r + j + 1) * P], ident[:, :])
                    tr.then_inc(z("turned"), 1)

                def values(h, tt):
                    pe.wait_ge(z("turn_lo"), 14 * h + (rounds(tt) + 1))
                    if not (isinstance(h, int) and h == 0 and tt == 0):
                        pe.wait_ge(z("o_written"), 8 * h + tt)
                    for j in range(tt + 1):
                        if j == 4:
                            pe.wait_ge(z("turn_lo"), 14 * h + (rounds(tt) + 2))
                        pe.matmul(bank(7)[:, 0:2 * P], g("PTH")[:, j, :], g("VHL")[:, j, :, :].rearrange("p a c -> p (a c)"),
                                  start=j == 0, stop=False)
                        mm = pe.matmul(bank(7)[:, 0:P], g("PTL")[:, j, :], g("VHL")[:, j, 0, :], start=False,
                                       stop=j == tt)
                    mm.then_inc(z("pv_done"), 1)

                def turn_o(h, tt):
                    pe.wait_ge(z("o_scaled"), 8 * h + tt + 1)
                    pe.transpose(bank(7)[:, 2 * P:3 * P], g("ot")[:, :], ident[:, :]).then_inc(z("o_turned"), 1)

                def head(h, nxt):
                    m = 0
                    for tt in range(NT + 1):
                        n = SHARE[tt] if nxt is not None and kind == "d" else 0
                        if tt < NT:
                            scores(h, tt)
                        if tt:
                            turn(h, tt - 1, 0)
                        else:
                            turn_v(h, 0)
                        a, b = (n * 2 // 5, n * 4 // 5) if 0 < tt < NT else (n // 2, n)
                        if tt >= 2:
                            turn_o(h, tt - 2)
                        proj(nxt, m, m + a)
                        if tt == 0 and not (isinstance(h, int) and h == 0):
                            turn_o(h - 1, NT - 1)
                        if tt > 4:
                            turn(h, tt - 1, 1)
                        if tt == 1:
                            turn_v(h, 1)
                        proj(nxt, m + a, m + b)
                        if tt:
                            values(h, tt - 1)
                        proj(nxt, m + b, m + n)
                        m += n

                if kind == "d":
                    project_arriving(2, b0)
                    proj(0, 96, 144)
                    pe.wait_ge(s["stage_end"], 3 * 7)
                head(0, 1)
                with pe.Fori(1, heads - 1) as h:
                    head(h, h + 1)
                head(heads - 1, None)
                turn_o(heads - 1, NT - 1)

            def out_projection(b0, first_k):
                for m in range(KT):
                    b = b0 + m
                    if m >= 2:
                        pe.wait_ge(s["out_added"], first_k + m - 1)
                    for half in range(2):
                        pe.wait_ge(s["w_split"], b + 1)
                        for k in range(KT):
                            if m == 0 and half == 0:
                                pe.wait_ge(s["o_split"], first_k + k + 1)
                            cs, ts = slice(k * P, k * P + P), slice(half * HALF, half * HALF + HALF)
                            mm = split_product(bank(2 * (m % 2) + half), WH[:, b % RING, cs], WL[:, b % RING, cs],
                                               HNH[:, k, ts], HNL[:, k, ts], k == 0, k == KT - 1)
                        mm.then_inc(s["first_half"] if half == 0 else s["blocks_freed"], 1)

            def feed_forward(layer, b0, norm_n):
                def up(n, pos, off):
                    start = isinstance(n, int) and n == 0
                    if start:
                        project_arriving(norm_n, pos)
                    for j in range(1 if start else 0, 2):
                        tile = 2 * n + (2 * GROUPS * layer + j)
                        for part, read, bk in ((0, "gate_taps", 0), (1, "gated", 2)):
                            pe.wait_ge(s[read], tile)
                            for half in range(2):
                                project(pos + (2 * j + part), (b0 + off + 2 * j + part) % RING, half, bank(bk + half))

                def down(n, pos, off, par):
                    pe.wait_ge(s["w_split"], pos + 2)
                    pe.wait_ge(s["hid_lo"], 2 * n + (2 * GROUPS * layer + 2))
                    for m in range(KT):
                        g = 8 * n + (8 * GROUPS * layer + m)
                        pe.wait_ge(s["down_added"], g + 1)
                        for half in range(2):
                            for j in range(2):
                                slot = (b0 + off + j) % RING
                                cs, ts = slice(m * P, m * P + P), slice(half * HALF, half * HALF + HALF)
                                mm = split_product(bank(4 + 2 * (m % 2) + half), WH[:, slot, cs], WL[:, slot, cs],
                                                   ffn["HH"][:, 2 * par + j, ts], ffn["HL"][:, 2 * par + j, ts],
                                                   j == 0, j == 1)
                        if m < KT - 1:
                            mm.then_inc(s["down_ready"], 1)
                        else:
                            mm.then_inc(s["blocks_freed"], 2)

                up(0, b0, 0)
                with pe.Fori(0, (GROUPS - 1) // 2) as i:
                    for q in range(2):
                        up(2 * i + (1 + q), 12 * i + (b0 + 4 + 6 * q), 4 + 6 * q)
                        down(2 * i + q, 12 * i + (b0 + 8 + 6 * q), 8 + 6 * q, q)
                down(GROUPS - 1, b0 + 6 * GROUPS - 2, 6 * GROUPS - 2, (GROUPS - 1) % 2)

            attention("f", fox, 1, H_FOX, B_FOX, 0)
            stage_end(pe, 4)
            out_projection(B_EVOUT, 0)
            stage_end(pe, 5)
            norm(1)
            feed_forward(0, B_FFN0, 1)
            stage_end(pe, 6)
            norm(2)
            stage_end(pe, 7, wait=False)
            attention("d", dif, 2, H_DIFF, B_DIFF, 0)
            stage_end(pe, 8)
            out_projection(B_ODOUT, 8)
            stage_end(pe, 9)
            norm(3)
            feed_forward(1, B_FFN1, 3)
            stage_end(pe, 10)
            norm(4)

        @block.scalar
        def _(act):
            link = Chain(act, s["act_chain"])
            silu = "silu_and_others"
            exp_ln = "natural_log_exp_and_others"

            def square(n, k):
                if k >= 2:
                    act.wait_ge(s["sq_added"], 8 * n + k - 1)
                act.activation(sqb[:, k % 2, :], X[:, k, :], ACT.Square).then_inc(s["sq_done"], 1)

            def norm(n):
                act.preload_act_table_set(exp_ln)
                act.wait_ge(s["sum_ready"], n + 1)
                link(act.activation(tok[:, 0:NT], bank(6)[:, 0:NT], ACT.Ln, bias=epsc[:, :], scale=1.0 / D))
                act.activation(tok[:, 0:NT], tok[:, 0:NT], ACT.Exp, scale=-0.5).then_inc(s["root_ready"], 1)
                if n < 4:
                    for k in range(KT):
                        act.wait_ge(s["hn_scaled"], 8 * n + k + 1)
                        act.activation(HNH[:, k, :], sqb[:, k % 2, :], ACT.Copy, scale=col(C_NORM + KT * n + k)).then_inc(
                            s["hn_hi"], 1)

            act.dma_start(ident[:, :], t["ident"]).then_inc(s["x_in"], 16)
            act.dma_start(dn["SC"][:, 0:P], t["mask"]).then_inc(s["x_in"], 16)
            act.dma_start(cols[:, :], t["cols"]).then_inc(s["consts_in"], 16)
            for part in range(KT // 2):
                act.dma_start(X[:, 2 * part:2 * part + 2, :],
                              t["xT"][2 * part * P:(2 * part + 2) * P, :].rearrange("(k p) n -> p k n", p=P)).then_inc(
                    x_part[part], 16)
            act.dma_start(dn["SELG"][:, :, :], t["selg"]).then_inc(s["rows_in"], 16)
            act.dma_start(dn["LM"][:, :, :], t["lm"]).then_inc(s["rows_in"], 16)
            act.dma_start(dn["MI"][:, :], t["mi"]).then_inc(s["rows_in"], 16)
            for k in range(KT):
                if k % 2 == 0:
                    act.wait_ge(x_part[k // 2], 16)
                square(0, k)
            act.wait_ge(s["consts_in"], 16)
            act.wait_ge(s["small_consts"], 1)
            norm(0)

            act.preload_act_table_set(silu)
            act.wait_ge(s["blocks_freed"], 1)
            act.wait_ge(s["hn_ready"], 8)
            act.dma_start(dnp["rst"][:, :], t["rst"]).then_inc(s["rst_in"], 16)
            act.activation(dnp["lg"][:, :], bank(0, 2), ACT.Copy).then_inc(s["conv_taps"], 1)
            for n in range(1, 13):
                act.wait_ge(s["blocks_freed"], n + 1)
                if n >= 3:
                    act.wait_ge(s["dn_silu"], n - 2)
                act.activation(dnp["dn_conv"][:, n % 2, :], bank(2 * (n % 3), 2), ACT.Copy,
                               scale=col(C_DNCONV + 4 * (n - 1) + 3)).then_inc(s["conv_start"], 1)
                act.wait_ge(s["conv_taps"], n + 1)
                if n >= 3:
                    act.wait_ge(dn_stored[n % 2], 16 * ((n - 1) // 2))
                act.activation(dnp["dn_out"][:, n % 2, :], dnp["dn_conv"][:, n % 2, :], ACT.Silu).then_inc(s["dn_silu"], 1)
                act.wait_ge(s["dn_silu"], n)
                act.dma_start(t["qkv"][n - 1, :, :], dnp["dn_out"][:, n % 2, :]).then_inc(dn_stored[n % 2], 16)
                if n == 3:
                    act.wait_ge(s["rows_y"], 1)
                    link(act.activation(dnp["lg_a"][:, :], dnp["lg"][:, :], ACT.Abs))
                    link(act.activation(dnp["lg_a"][:, :], dnp["lg_a"][:, :], ACT.Exp, scale=-1.0))
                    act.activation(dnp["lg_a"][:, :], dnp["lg_a"][:, :], ACT.Ln, bias=ones[:, 0:1]).then_inc(s["rows_l"], 1)
                    act.activation(small[:, 0:1], col(C_ROW + 2), ACT.Exp).then_inc(s["rows_l"], 1)
                if n == 9:
                    for r in range(2):
                        act.wait_ge(s["rows_turned"], r + 1)
                        act.activation(dn["TKN"][:, 4 * r:4 * r + 4, :].rearrange("p t c -> p (t c)"), bank(6 + r), ACT.Copy,
                                       scale=-1.0).then_inc(s["rows_kept"], 1)
                if n == 10:
                    act.wait_ge(s["rows_kept"], 2)
                    act.activation(dn["TE"][:, :, :].rearrange("p t c -> p (t c)"),
                                   dn["TKN"][:, :, :].rearrange("p t c -> p (t c)"), ACT.Exp, scale=-1.0).then_inc(
                        s["te_ready"], 1)
                    act.wait_ge(s["rows_turned"], 3)
                    act.activation(dn["GLB"][:, :, :].rearrange("p h c -> p (h c)"), bank(6)[:, 0:64], ACT.Exp).then_inc(
                        s["te_ready"], 1)
            def keep(e, half, bk):
                act.wait_ge(s["first_half"] if half == 0 else s["blocks_freed"], e + (B_Z + 1))
                if not (isinstance(e, int) and e == 0):
                    act.wait_ge(kept_stored[half], 16 * e)
                act.activation(PJ[:, half, :], bank(bk), ACT.Copy).then_inc(s["kept_written"], 1)

            keep(0, 0, 2)
            keep(0, 1, 3)
            for q in range(2):
                act.wait_ge(dn_stored[q], 16 * 6)
            stage_end(act, 1)

            d = dn
            flat = lambda a: a[:, :, :].rearrange("p h c -> p (h c)")

            def load_tile(i):
                qkv = t["qkv"].rearrange("(a h) p n -> a p h n", a=3)
                for a, n in enumerate(("qs", "ks", "vs")):
                    act.dma_start(d[n][:, :, :], qkv[a, :, :, bass.ts(i, P)]).then_inc(s["dn_loaded"], 16)

            def token_tile(i, busy, last=False):
                def beside(j):
                    if busy:
                        keep(BESIDE * i + (1 + j // 2), j % 2, j % 2)

                act.wait_ge(s["dn_turn1"], i + 1)
                act.activation(flat(d["u"]), bank(2), ACT.Square).then_inc(s["dn_square"], 1)
                act.activation(flat(d["wT"]), bank(3), ACT.Square).then_inc(s["dn_square"], 1)
                act.wait_ge(s["dn_ss"], i + 1)
                link(act.activation(small[:, 16:24], small[:, 8:16], ACT.Ln, bias=epsc[:, :]))
                act.activation(small[:, 16:24], small[:, 16:24], ACT.Exp, scale=-0.5).then_inc(s["dn_root"], 1)
                for n, (dst, bk) in enumerate(((d["knT"][:, :, :], 5), (d["kbqT"][:, :, 0, :], 6),
                                               (d["kbqT"][:, :, 1, :], 7), (d["qgT"][:, :, :], 2))):
                    act.wait_ge(s["dn_turn2"], 4 * i + n + 1)
                    act.activation(dst, bank(bk).rearrange("p (h c) -> p h c", h=4), ACT.Copy).then_inc(s["dn_evac2"], 1)
                beside(0)
                act.wait_ge(s["dn_dec"], i + 1)
                act.activation(flat(d["dec"]), flat(d["dec"]), ACT.Exp).then_inc(s["dn_exp"], 1)
                if last:
                    act.preload_act_table_set(silu)
                    act.wait_ge(s["z_in"], 16)
                beside(1)
                for lv in range(1, LEVELS):
                    act.wait_ge(s["dn_y"], (LEVELS - 1) * i + lv)
                    act.activation(flat(d["sq"]), bank(7), ACT.Copy).then_inc(s["dn_yc"], 1)
                    if lv in (2, 4):
                        beside(1 + lv // 2)
                    if last and lv <= H_DN:
                        act.activation(X[:, H_DN + lv - 1, :], X[:, H_DN + lv - 1, :], ACT.Silu).then_inc(s["z_silu"], 1)
                if last:
                    act.preload_act_table_set(exp_ln)
                act.wait_ge(s["dn_uw"], 2 * i + 2)
                act.activation(flat(d["wT"]), bank(4), ACT.Copy).then_inc(s["dn_wc"], 1)
                if not last:
                    load_tile(i + 1)
                beside(4)
                act.wait_ge(s["dn_o"], 2 * i + 2)
                act.activation(flat(d["sq"]), bank(7), ACT.Square).then_inc(s["dn_osq"], 1)
                act.wait_ge(s["dn_oss"], i + 1)
                link(act.activation(small[:, 28:32], small[:, 24:28], ACT.Ln, bias=epsc[:, :], scale=1.0 / P))
                act.activation(small[:, 28:32], small[:, 28:32], ACT.Exp, scale=-0.5).then_inc(s["dn_ort"], 1)
                beside(5)
                act.wait_ge(s["dn_ot"], i + 1)
                act.activation(X[:, 0:4, bass.ts(i, P)], bank(5).rearrange("p (h c) -> p h c", h=4), ACT.Copy,
                               scale=col(C_DNW)).then_inc(s["dn_ow"], 1)

            load_tile(0)
            act.preload_act_table_set(exp_ln)
            with act.Fori(0, BUSY_TILES) as i:
                link.enter(i, 2)
                token_tile(i, True)
            link.leave(BUSY_TILES)
            with act.Fori(BUSY_TILES, NT - 1) as i:
                link.enter(i, 2, BUSY_TILES)
                token_tile(i, False)
            link.leave(NT - 1 - BUSY_TILES)
            token_tile(NT - 1, False, last=True)
            stage_end(act, 2)

            stage_end(act, 3)

            def attention(kind, buf, maps, heads, b0, half0, o_tile, links):
                z = lambda n: s[f"{kind}_{n}"]
                g = lambda n: buf[f"{kind}_{n}"]
                scale = DH ** -0.5 if kind == "d" else P ** -0.5

                def evacuate(hp, j):
                    if j % 2 == 0:
                        act.wait_ge(s["first_half"], 3 * hp + (half0 + j // 2 + 1))
                    else:
                        act.wait_ge(s["blocks_freed"], 3 * hp + (b0 + j // 2 + 1))
                    dst = g(("rawq", "rawk", "rawv")[j // 2])[:, (j % 2) * HALF:(j % 2 + 1) * HALF]
                    b = j if isinstance(hp, int) and hp == 0 and j < 4 else j % 2
                    act.activation(dst, bank(b), ACT.Copy, scale=scale if j < 2 else 1.0).then_inc(
                        z("raw_written"), 1)

                def qk_high(h, which):
                    name, raw = ("QH", "rawq") if which == 0 else ("KH", "rawk")
                    if which == 0 and kind == "d":
                        act.wait_ge(z("roped"), 2 * h + 2)
                    elif which == 0:
                        act.wait_ge(z("raw_in"), 48 * h + 48)
                    act.activation(g(name)[:, :], g(raw)[:, :], ACT.Copy,
                                   scale=scale if kind == "f" and which == 0 else 1.0).then_inc(z("qk_hi"), 1)

                def o_root(h, tt):
                    if kind == "d":
                        act.wait_ge(z("o_summed"), 8 * h + tt + 1)
                        act.activation(bank(7)[:, 3 * P:4 * P], g("ot")[:, :], ACT.Square,
                                       accum_out=buf["dsc"][:, 0:1]).then_inc(z("squared"), 1)
                        act.wait_ge(z("squared"), 8 * h + tt + 1)
                        link(act.activation(buf["dsc"][:, 2:3], buf["dsc"][:, 0:1], ACT.Ln, scale=1.0 / P,
                                            bias=epsc[:, :]))
                        act.activation(buf["dsc"][:, 2:3], buf["dsc"][:, 2:3], ACT.Exp, scale=-0.5).then_inc(
                            z("rootd"), 1)

                def o_write(h, tt):
                    act.wait_ge(z("o_turned"), 8 * h + tt + 1)
                    act.activation(X[:, o_tile + h, tt * P:(tt + 1) * P], bank(7)[:, 2 * P:3 * P], ACT.Copy,
                                   scale=small[:, 40:41] if kind == "d" else 1.0).then_inc(z("o_written"), 1)

                def turned_high(h, tt, r):
                    act.wait_ge(z("turned"), 14 * h + (rounds(tt) + r + 1))
                    if r == 0 and tt:
                        act.wait_ge(z("pv_done"), 8 * h + tt)
                    c = min(4, tt + 1 - 4 * r)
                    act.activation(g("PTH")[:, 4 * r:4 * r + c, :],
                                   bank(6)[:, 0:c * P].rearrange("p (j c) -> p j c", j=c), ACT.Copy).then_inc(
                        z("turn_hi"), 1)

                def exponent(h, tt, m):
                    n = P * (tt + 1)
                    if m == 0 and tt >= 2:
                        act.wait_ge(z("turned"), 14 * h + rounds(tt - 1))
                    act.wait_ge(z("max_ready"), (8 * h + tt) * maps + m + 1)
                    act.activation(g("e0")[:, tt % 2, 0:n] if m == 0 else buf["e1"][:, 0:n], bank(2 + 2 * m, 2)[:, 0:n],
                                   ACT.Exp, bias=g("nmax")[:, m:m + 1],
                                   accum_out=g("sums")[:, tt % 2, m:m + 1]).then_inc(z("exped"), 1)

                def v_high(h, r):
                    act.wait_ge(z("turned"), 14 * h + V_ROUNDS[r] + 1)
                    act.activation(g("VHL")[:, 4 * r:4 * r + 4, 0, :], bank(6).rearrange("p (j c) -> p j c", j=4),
                                   ACT.Copy).then_inc(z("turn_hi"), 1)

                def head(h, nxt):
                    for tt in range(NT + 1):
                        if tt >= 2:
                            o_root(h, tt - 2)
                        elif tt == 0 and not (isinstance(h, int) and h == 0):
                            o_root(h - 1, NT - 1)
                        if tt:
                            turned_high(h, tt - 1, 0)
                        else:
                            v_high(h, 0)
                        if tt >= 2:
                            o_write(h, tt - 2)
                        elif tt == 0 and not (isinstance(h, int) and h == 0):
                            o_write(h - 1, NT - 1)
                        if tt < NT:
                            exponent(h, tt, 0)
                        if tt > 4:
                            turned_high(h, tt - 1, 1)
                        if tt < NT and maps == 2:
                            exponent(h, tt, 1)
                        if tt == 1:
                            v_high(h, 1)
                        if nxt is not None:
                            if tt == 0 and kind == "d":
                                act.wait_ge(z("qk_lo"), 2 * h + 2)
                            for j in HALVES_DONE[tt] if kind == "d" else ():
                                evacuate(nxt, j)
                            if tt == NT - 1:
                                qk_high(nxt, 0)
                                qk_high(nxt, 1)

                for j in range(6) if kind == "d" else ():
                    evacuate(0, j)
                act.preload_act_table_set(exp_ln)
                qk_high(0, 0)
                qk_high(0, 1)
                head(0, 1)
                with act.Fori(1, heads - 1) as h:
                    link.enter(h, links, 1)
                    head(h, h + 1)
                link.leave(heads - 2)
                head(heads - 1, None)
                o_root(heads - 1, NT - 1)
                o_write(heads - 1, NT - 1)

            def out_projection(x_src, first, norm_n):
                for k in range(KT):
                    act.activation(HNH[:, k, :], X[:, k, :], ACT.Copy).then_inc(s["o_hi"], 1)
                for m in range(KT):
                    if m >= 2:
                        act.wait_ge(s["out_added"], first + m - 1)
                    act.dma_start(ost["xt"][:, m % 2, :], x_src[m * P:(m + 1) * P, :]).then_inc(s["x_back"], 16)
                    act.wait_ge(s["x_back"], 16 * (first + m + 1))
                    if m >= 2:
                        square(norm_n, m - 2)
                for k in range(KT - 2, KT):
                    act.wait_ge(s["out_added"], first + k + 1)
                    square(norm_n, k)

            def feed_forward(layer, b0):
                def tile(n, j, pos, par):
                    g = 2 * n + (2 * GROUPS * layer + j)
                    act.wait_ge(s["blocks_freed"], pos + (2 * j + 1))
                    act.wait_ge(s["params_in"], n + (GROUPS * layer + 1))
                    if not (isinstance(n, int) and n == 0 and j == 0 and layer == 0):
                        act.wait_ge(s["gated"], g)
                    act.activation(cv[:, j, :], bank(0, 2), ACT.Identity, scale=ffn["fp"][:, j, 2:3],
                                   bias=ffn["fp"][:, j, 3:4]).then_inc(s["gate_mid"], 1)
                    act.wait_ge(s["gate_taps"], g + 1)
                    act.activation(cv[:, j, :], cv[:, j, :], ACT.Silu).then_inc(s["silu_done"], 1)
                    act.wait_ge(s["gated"], g + 1)
                    act.activation(ffn["HH"][:, 2 * par + j, :], ffn["hb"][:, :], ACT.Copy).then_inc(s["hid_hi"], 1)

                act.preload_act_table_set(silu)
                for j in range(2):
                    tile(0, j, b0, 0)
                with act.Fori(0, (GROUPS - 1) // 2) as i:
                    for q in range(2):
                        for j in range(2):
                            tile(2 * i + (1 + q), j, 12 * i + (b0 + 4 + 6 * q), (1 + q) % 2)
                for k in range(KT):
                    act.wait_ge(s["down_added"], 8 * GROUPS * layer + 8 * (GROUPS - 1) + k + 3)
                    square(2 * layer + 2, k)

            act.dma_start(fox["SELC"][:, :, :], t["selc"]).then_inc(s["rows_in"], 16)
            attention("f", fox, 1, H_FOX, B_FOX, B_FOX, 4, 0)
            stage_end(act, 4)
            out_projection(t["xT"], 0, 1)
            stage_end(act, 5)
            norm(1)
            feed_forward(0, B_FFN0)
            stage_end(act, 6)
            act.dma_start(t["spill"].rearrange("(k p) n -> p k n", p=P), X[:, :, :]).then_inc(s["spilled"], 16)
            norm(2)
            act.wait_ge(s["spilled"], 16)
            stage_end(act, 7)
            act.dma_start(dif["cosT"][:, :], t["cosT"]).then_inc(s["spilled"], 16)
            act.dma_start(dif["sinT"][:, :], t["sinT"]).then_inc(s["spilled"], 16)
            act.wait_ge(s["spilled"], 48)
            act.wait_ge(s["rows_scan"], 4)
            act.activation(small[:, 44:46], small[:, 42:44], ACT.Exp).then_inc(s["rows_l"], 1)
            attention("d", dif, 2, H_DIFF, B_DIFF, B_DIFF - FT, 0, NT)
            stage_end(act, 8)
            out_projection(t["spill"], 8, 3)
            stage_end(act, 9)
            norm(3)
            feed_forward(1, B_FFN1)
            stage_end(act, 10)
            norm(4)

        @block.vector
        def _(dve):
            link = Chain(dve, s["dve_chain"])

            def add_square(n, k):
                dve.wait_ge(s["sq_done"], 8 * n + k + 1)
                if k == 0:
                    op = dve.tensor_copy(acc[:, :], sqb[:, 0, :])
                else:
                    dve.wait_ge(s["sq_added"], 8 * n + k)
                    op = dve.tensor_tensor(acc[:, :], acc[:, :], sqb[:, k % 2, :], ALU.add)
                op.then_inc(s["sq_added"], 1)

            def norm(n):
                y, x, step = (tok[:, a * NT:a * NT + NT] for a in range(3))
                dve.wait_ge(s["root_ready"], n + 1)
                link(dve.tensor_scalar(x, bank(6)[:, 0:NT], 1.0 / D, EPS, ALU.mult, ALU.add))
                link(dve.tensor_tensor(step, y, y, ALU.mult))
                link(dve.tensor_tensor(step, step, x, ALU.mult))
                link(dve.tensor_scalar(step, step, -0.5, 1.5, ALU.mult, ALU.add))
                link(dve.tensor_tensor(y, y, step, ALU.mult))
                dve.tensor_tensor(rt[:, :].rearrange("p (t c) -> p t c", t=NT), ident[:, :].unsqueeze(1).to_broadcast([P, NT, P]),
                                  y.unsqueeze(2).to_broadcast([P, NT, P]), ALU.mult).then_inc(s["diagonal"], 1)
                dve.wait_ge(s["spread"], n + 1)
                if n < 4:
                    def scaled(k):
                        if k >= 2:
                            dve.wait_ge(s["hn_ready"], 8 * n + k - 1)
                        dve.tensor_tensor(sqb[:, k % 2, :], X[:, k, :], bank(6, 2), ALU.mult).then_inc(s["hn_scaled"], 1)

                    scaled(0)
                    for k in range(KT):
                        if k + 1 < KT:
                            scaled(k + 1)
                        dve.wait_ge(s["hn_hi"], 8 * n + k + 1)
                        dve.scalar_tensor_tensor(out=HNL[:, k, :], in0=sqb[:, k % 2, :], scalar=col(C_NORM + KT * n + k),
                                                 in1=HNH[:, k, :], op0=ALU.mult, op1=ALU.subtract).then_inc(
                            s["hn_ready"], 1)
                else:
                    for k in range(KT):
                        dve.scalar_tensor_tensor(out=X[:, k, :], in0=X[:, k, :], scalar=col(C_NORM + KT * n + k),
                                                 in1=bank(6, 2), op0=ALU.mult, op1=ALU.mult).then_inc(s["out_scaled"], 1)

            link(dve.memset(ones[:, :], 1.0))
            link(dve.memset(epsc[:, :], EPS))
            link(dve.memset(small[:, :], 0.0))
            dve.memset(small[:, 1:2], 0.0).then_inc(s["down_added"], 2)
            dve.wait_ge(s["consts_in"], 16)
            dve.wait_ge(s["x_in"], 32)
            link(dve.tensor_copy(identb[:, :], ident[:, :]))
            dve.tensor_copy(maskb[:, :], dn["SC"][:, 0:P]).then_inc(s["small_consts"], 1)
            for k in range(KT):
                add_square(0, k)
            norm(0)

            for n in range(1, 13):
                dve.wait_ge(s["conv_start"], n)
                buf, src = dnp["dn_conv"][:, n % 2, :], bank(2 * (n % 3), 2)
                for back in range(1, 4):
                    op = dve.scalar_tensor_tensor(out=buf[:, back:S], in0=src[:, 0:S - back],
                                                  scalar=col(C_DNCONV + 4 * (n - 1) + 3 - back), in1=buf[:, back:S],
                                                  op0=ALU.mult, op1=ALU.add)
                    if back < 3:
                        link(op)
                    else:
                        op.then_inc(s["conv_taps"], 1)
                if n == 3:
                    dve.wait_ge(s["conv_taps"], n + 1)
                    lg, la, lb = dnp["lg"], dnp["lg_a"], dnp["lg_b"]
                    dve.tensor_scalar(lg[:, :], lg[:, :], col(C_ROW + 1), col(C_ROW), ALU.add, ALU.mult).then_inc(s["rows_y"], 1)
                    dve.wait_ge(s["rows_l"], 2)
                    link(dve.scalar_tensor_tensor(out=lb[:, :], in0=lg[:, :], scalar=0.0, in1=la[:, :], op0=ALU.max, op1=ALU.add))
                    link(dve.tensor_scalar(lb[:, :], lb[:, :], small[:, 0:1], -1.0, ALU.mult, ALU.mult))
                    SC = dn["SC"]
                    dve.wait_ge(s["rst_in"], 16)
                    dve.tensor_tensor_scan(lg[:, :], dnp["rst"][:, :], lb[:, :], 0.0, ALU.mult, ALU.add).then_inc(s["rows_scan"], 1)
                    dve.wait_ge(s["rows_scan"], 1)
                    link(dve.tensor_copy(la[:, :], lg[:, :]))
                    g_rows = la[R_G:R_G + 32, :].rearrange("p (n c) -> p n c", c=CHUNK)
                    link(dve.tensor_tensor(
                        la[R_TAIL:R_TAIL + 32, :].rearrange("p (n c) -> p n c", c=CHUNK),
                        g_rows[:, :, CHUNK - 1:CHUNK].to_broadcast([32, S // CHUNK, CHUNK]), g_rows, ALU.subtract))
                    link(dve.memset(CHL[:, :].bitcast(F32), 0.0))
                    link(dve.tensor_copy(CHL[R_F:R_F + 4, :], lg[R_F:R_F + 4, :]))
                    link(dve.tensor_tensor(lb[R_F:R_F + 4, :], lg[R_F:R_F + 4, :], CHL[R_F:R_F + 4, :], ALU.subtract))
                    link(dve.tensor_copy(CHL[R_TAIL:R_TAIL + 4, :], lb[R_F:R_F + 4, :]))
                    dve.tensor_copy(SC[:, :], la[:, :]).then_inc(s["rows_scan"], 1)
            dve.wait_ge(s["te_ready"], 2)
            for h in range(4):
                dve.memset(dn["St"][:, h, :], 0.0).then_inc(s["dn_sc"], 1)
            dve.wait_ge(s["dn_sc"], 4)
            stage_end(dve, 1)

            d = dn
            b4 = lambda a: bank(a).rearrange("p (h c) -> p h c", h=4)
            wide = lambda c: c.unsqueeze(2).to_broadcast([P, 4, P])
            with dve.Fori(0, NT) as i:
                link.enter(i, 23)
                link(dve.tensor_copy(d["te"][:, :], d["TE"][:, i, :]))
                link(dve.tensor_copy(d["tkn"][:, :], d["TKN"][:, i, :]))
                link(dve.tensor_copy(d["glt"][:, :, :], d["GLB"][:, :, bass.ts(i, 2)]))
                beta, eg, tail = (d["te"][:, r:r + 4] for r in (R_BETA, R_G, R_TAIL))
                dve.wait_ge(s["dn_square"], 2 * i + 2)
                link(dve.tensor_reduce(small[:, 8:12], d["u"][:, :, :], AX.X, ALU.add))
                dve.tensor_reduce(small[:, 12:16], d["wT"][:, :, :], AX.X, ALU.add).then_inc(s["dn_ss"], 1)
                dve.wait_ge(s["dn_root"], i + 1)

                def newton(y, x, tmp, add, mul):
                    link(dve.tensor_scalar(tmp, x, mul, add, ALU.mult, ALU.add))
                    link(dve.tensor_tensor(tmp, tmp, y, ALU.mult))
                    link(dve.tensor_tensor(tmp, tmp, y, ALU.mult))
                    link(dve.tensor_scalar(tmp, tmp, -0.5, 1.5, ALU.mult, ALU.add))
                    link(dve.tensor_tensor(y, y, tmp, ALU.mult))

                newton(small[:, 16:24], small[:, 8:16], small[:, 32:40], EPS, 1.0)
                rk, rq = small[:, 16:20], small[:, 20:24]
                fb, fbg, fd, fg = (small[:, c:c + 4] for c in (48, 52, 56, 60))
                link(dve.tensor_scalar(rq, rq, P ** -0.5, None, ALU.mult))
                link(dve.tensor_tensor(fb, rk, beta, ALU.mult))
                link(dve.tensor_tensor(fbg, fb, eg, ALU.mult))
                link(dve.tensor_tensor(fd, rk, tail, ALU.mult))
                link(dve.tensor_tensor(fg, rq, eg, ALU.mult))
                for n, bk, f in (("kn", 2, rk), ("kb", 2, fb), ("qn", 3, rq), ("qg", 3, fg), ("kbg", 2, fbg),
                                 ("kd", 2, fd), ("vb", 4, beta)):
                    dve.tensor_tensor(d[n][:, :, :], b4(bk), wide(f), ALU.mult).then_inc(s["dn_scale"], 1)
                dve.wait_ge(s["dn_pair"], 2 * i + 2)
                link(dve.tensor_tensor(d["dec"][:, :, :], b4(5), wide(d["tkn"][:, R_G:R_G + 4]), ALU.add))
                dve.tensor_scalar(d["dec"][:, :, :], d["dec"][:, :, :], 0.0, None, ALU.min).then_inc(s["dn_dec"], 1)
                dve.wait_ge(s["dn_exp"], i + 1)
                link(dve.tensor_tensor(d["dec"][:, :, :], d["dec"][:, :, :],
                                       d["MI"][:, :].unsqueeze(1).to_broadcast([P, 4, P]), ALU.mult))
                pair = bank(3, 2).rearrange("p (h a c) -> p h a c", h=4, a=2)
                link(dve.tensor_tensor(d["LT"][:, :, :], pair[:, :, 0, :], d["dec"][:, :, :], ALU.mult))
                dve.tensor_tensor(d["QKT"][:, :, :], pair[:, :, 1, :], d["dec"][:, :, :], ALU.mult).then_inc(
                    s["dn_mask"], 2)

                def level(lv):
                    dst = d["kn"] if lv == 0 else d[["kn", "kb"][lv % 2]]
                    return dve.tensor_tensor(dst[:, :, :], d["LT"][:, :, :],
                                             d["LM"][:, lv, :].unsqueeze(1).to_broadcast([P, 4, P]), ALU.mult)

                id4 = ident[:, :].unsqueeze(1).to_broadcast([P, 4, P])
                level(0).then_inc(s["dn_lts"], 1)
                level(1).then_inc(s["dn_lts"], 1)
                dve.wait_ge(s["dn_lts"], LEVELS * i + 1)
                dve.tensor_tensor(d["vs"][:, :, :], d["kn"][:, :, :], id4, ALU.add).then_inc(s["dn_xc"], 1)
                dve.wait_ge(s["dn_x1t"], i + 1)
                dve.tensor_tensor(d["qs"][:, :, :], b4(6), id4, ALU.add).then_inc(s["dn_xc"], 1)
                for lv in range(1, LEVELS):
                    dve.wait_ge(s["dn_xc"], 11 * i + 2 * lv)
                    if lv + 1 < LEVELS:
                        level(lv + 1).then_inc(s["dn_lts"], 1)
                    dve.wait_ge(s["dn_p"], 9 * i + (2 * lv - 1 if lv == LEVELS - 1 else 2 * lv))
                    dve.tensor_tensor(d["vs"][:, :, :], d["vs"][:, :, :], b4(2), ALU.add).then_inc(s["dn_xc"], 1)
                    if lv < LEVELS - 1:
                        dve.tensor_tensor(d["qs"][:, :, :], d["qs"][:, :, :], b4(5), ALU.add).then_inc(s["dn_xc"], 1)
                dve.wait_ge(s["dn_uw"], 2 * i + 1)
                link(dve.tensor_copy(d["u"][:, :, :], b4(3)))
                for c in range(2):
                    r = slice(c * CHUNK, c * CHUNK + CHUNK)
                    dve.wait_ge(s["dn_ws"], 2 * i + c + 1)
                    dve.tensor_tensor(d["vn"][r, :, :], d["u"][r, :, :], b4(6)[r, :, :], ALU.subtract).then_inc(
                        s["dn_vn"], 1)
                    dve.wait_ge(s["dn_s"], 2 * i + c + 1)
                    for h in range(4):
                        dve.scalar_tensor_tensor(out=d["St"][:, h, :], in0=d["St"][:, h, :], scalar=d["glt"][:, h, c:c + 1],
                                                 in1=b4(2)[:, h, :], op0=ALU.mult, op1=ALU.add).then_inc(s["dn_sc"], 1)
                    dve.wait_ge(s["dn_sc"], 8 * i + 8 + 4 * c)
                dve.wait_ge(s["dn_osq"], i + 1)
                dve.tensor_reduce(small[:, 24:28], d["sq"][:, :, :], AX.X, ALU.add).then_inc(s["dn_oss"], 1)
                dve.wait_ge(s["dn_ort"], i + 1)
                newton(small[:, 28:32], small[:, 24:28], small[:, 32:36], EPS, 1.0 / P)
                dve.tensor_tensor(d["dec"][:, :, :], b4(7), wide(small[:, 28:32]), ALU.mult).then_inc(s["dn_on"], 1)
            link.leave(NT)
            stage_end(dve, 2)

            for n in range(H_DN):
                dve.wait_ge(s["z_silu"], n + 1)
                dve.tensor_tensor(X[:, n, :], X[:, n, :], X[:, H_DN + n, :], ALU.mult).then_inc(s["z_done"], 1)
            stage_end(dve, 3)

            def attention(kind, buf, maps, heads, links):
                z = lambda n: s[f"{kind}_{n}"]
                g = lambda n: buf[f"{kind}_{n}"]

                def qk_low(h, which):
                    hi, lo, raw = (("QH", "QL", "rawq"), ("KH", "KL", "rawk"))[which]
                    dve.wait_ge(z("qk_hi"), 2 * h + which + 1)
                    if which == 0 and kind == "f":
                        op = dve.scalar_tensor_tensor(out=g(lo)[:, :], in0=g(raw)[:, :], scalar=P ** -0.5, in1=g(hi)[:, :],
                                                      op0=ALU.mult, op1=ALU.subtract)
                    else:
                        op = dve.tensor_tensor(g(lo)[:, :], g(raw)[:, :], g(hi)[:, :], ALU.subtract)
                    op.then_inc(z("qk_lo"), 1)

                def o_scale(h, tt):
                    ri = g("rinv")[:, tt % 4:tt % 4 + 1]
                    dve.wait_ge(z("pv_done"), 8 * h + tt + 1)
                    if tt or not (isinstance(h, int) and h == 0):
                        dve.wait_ge(z("o_turned"), 8 * h + tt)
                    link(dve.tensor_scalar(g("ot")[:, :], bank(7)[:, 0:P], ri, None, ALU.mult))
                    dve.scalar_tensor_tensor(out=g("ot")[:, :], in0=bank(7)[:, P:2 * P], scalar=ri, in1=g("ot")[:, :],
                                             op0=ALU.mult, op1=ALU.add).then_inc(
                        z("o_summed" if kind == "d" else "o_scaled"), 1)
                    if kind == "d":
                        dve.wait_ge(z("squared"), 8 * h + tt + 1)
                        dve.tensor_scalar(buf["dsc"][:, 1:2], buf["dsc"][:, 0:1], 1.0 / P, EPS, ALU.mult, ALU.add).then_inc(
                            z("ss_ready"), 1)
                        x, y, w = buf["dsc"][:, 1:2], buf["dsc"][:, 2:3], buf["dsc"][:, 3:4]
                        dve.wait_ge(z("ss_ready"), 8 * h + tt + 1)
                        dve.wait_ge(z("rootd"), 8 * h + tt + 1)
                        link(dve.tensor_scalar(w, y, y, x, ALU.mult, ALU.mult))
                        link(dve.tensor_scalar(w, w, -0.5, 1.5, ALU.mult, ALU.add))
                        dve.tensor_scalar(g("ot")[:, :], g("ot")[:, :], w, y, ALU.mult, ALU.mult).then_inc(z("o_scaled"), 1)

                def maximum(h, tt, m):
                    dve.wait_ge(z("scored"), (8 * h + tt) * maps + m + 1)
                    nm = g("nmax")[:, m:m + 1]
                    dve.tensor_reduce(nm, bank(2 + 2 * m, 2)[:, 0:P * (tt + 1)], AX.X, ALU.max, negate=True).then_inc(
                        z("max_ready"), 1)

                def turned_low(h, tt, r):
                    dve.wait_ge(z("turn_hi"), 14 * h + (rounds(tt) + r + 1))
                    c = min(4, tt + 1 - 4 * r)
                    dve.tensor_tensor(g("PTL")[:, 4 * r:4 * r + c, :],
                                      bank(6)[:, 0:c * P].rearrange("p (j c) -> p j c", j=c),
                                      g("PTH")[:, 4 * r:4 * r + c, :], ALU.subtract).then_inc(z("turn_lo"), 1)

                def v_low(h, r):
                    dve.wait_ge(z("turn_hi"), 14 * h + V_ROUNDS[r] + 1)
                    dve.tensor_tensor(g("VHL")[:, 4 * r:4 * r + 4, 1, :], bank(6).rearrange("p (j c) -> p j c", j=4),
                                      g("VHL")[:, 4 * r:4 * r + 4, 0, :], ALU.subtract).then_inc(z("turn_lo"), 1)

                def combine(h, tt):
                    n = P * (tt + 1)
                    dve.wait_ge(z("exped"), (8 * h + tt) * maps + 1)
                    su = lambda m: g("sums")[:, tt % 2, m:m + 1]
                    link(dve.reciprocal(g("rinv")[:, tt % 4:tt % 4 + 1], su(0)))
                    if kind == "d":
                        w = buf["dsc"][:, 4:5]
                        dve.wait_ge(z("exped"), (8 * h + tt + 1) * maps)
                        link(dve.reciprocal(w, su(1)))
                        link(dve.tensor_scalar(w, w, su(0), small[:, 41:42], ALU.mult, ALU.mult))
                        dve.scalar_tensor_tensor(out=g("e0")[:, tt % 2, 0:n], in0=buf["e1"][:, 0:n], scalar=w,
                                                 in1=g("e0")[:, tt % 2, 0:n], op0=ALU.mult, op1=ALU.add).then_inc(
                            z("combined"), 1)

                def head(h, nxt):
                    if kind == "f":
                        dve.tensor_copy(buf["selc"][:, :], buf["SELC"][:, h, :]).then_inc(z("sel_ready"), 1)
                    for tt in range(NT + 1):
                        if tt >= 2:
                            o_scale(h, tt - 2)
                        elif tt == 0 and not (isinstance(h, int) and h == 0):
                            o_scale(h - 1, NT - 1)
                        if tt == 0:
                            v_low(h, 0)
                        if tt < NT:
                            maximum(h, tt, 0)
                        if tt:
                            turned_low(h, tt - 1, 0)
                        if tt < NT and maps == 2:
                            maximum(h, tt, 1)
                        if tt > 4:
                            turned_low(h, tt - 1, 1)
                        if tt == 1:
                            v_low(h, 1)
                        if tt < NT:
                            combine(h, tt)
                        if kind == "f" and nxt is not None and tt == NT - 1:
                            qk_low(nxt, 0)
                            qk_low(nxt, 1)

                if kind == "d":
                    for which, (sw, name, raw) in enumerate((("e1", "swapped_q", "rawq"), ("xs", "swapped_k", "rawk"))):
                        dve.wait_ge(z(name), 64)
                        link(dve.tensor_tensor(buf[sw][:, :], buf[sw][:, :], buf["sinT"][:, :], ALU.mult))
                        link(dve.tensor_tensor(g(raw)[:, :], g(raw)[:, :], buf["cosT"][:, :], ALU.mult))
                        dve.tensor_tensor(g(raw)[:, :], g(raw)[:, :], buf[sw][:, :], ALU.add).then_inc(z("roped"), 1)
                qk_low(0, 0)
                qk_low(0, 1)
                head(0, 1)
                with dve.Fori(1, heads - 1) as h:
                    link.enter(h, links, 1)
                    head(h, h + 1)
                link.leave(heads - 2)
                head(heads - 1, None)
                o_scale(heads - 1, NT - 1)

            def out_projection(b0, first, norm_n):
                for k in range(KT):
                    dve.wait_ge(s["o_hi"], first + k + 1)
                    dve.tensor_tensor(HNL[:, k, :], X[:, k, :], HNH[:, k, :], ALU.subtract).then_inc(s["o_split"], 1)
                dve.wait_ge(s["o_split"], first + KT)
                for m in range(KT):
                    dve.wait_ge(s["blocks_freed"], b0 + m + 1)
                    dve.wait_ge(s["x_back"], 16 * (first + m + 1))
                    dve.tensor_tensor(X[:, m, :], bank(2 * (m % 2), 2), ost["xt"][:, m % 2, :], ALU.add).then_inc(
                        s["out_added"], 1)
                    if m:
                        add_square(norm_n, m - 1)
                add_square(norm_n, KT - 1)

            def feed_forward(layer, b0, links):
                def params(n):
                    at = C_FFN + layer * FT * 4
                    if isinstance(n, int):
                        src = cols[:, at + 8 * n:at + 8 * n + 8]
                    else:
                        src = cols[:, bass.ds(n * 8 + at, 8)]
                    dve.tensor_copy(ffn["fp"][:, :, :].rearrange("p a b -> p (a b)"), src).then_inc(s["params_in"], 1)

                def tile(n, j, pos, par):
                    g = 2 * n + (2 * GROUPS * layer + j)
                    dve.wait_ge(s["gate_mid"], g + 1)
                    c, ga = cv[:, j, :], bank(0, 2)
                    for back in (1, 2):
                        op = dve.scalar_tensor_tensor(out=c[:, back:S], in0=ga[:, 0:S - back],
                                                      scalar=ffn["fp"][:, j, 2 - back:3 - back], in1=c[:, back:S],
                                                      op0=ALU.mult, op1=ALU.add)
                        if back == 1:
                            link(op)
                        else:
                            op.then_inc(s["gate_taps"], 1)
                    dve.wait_ge(s["silu_done"], g + 1)
                    dve.wait_ge(s["blocks_freed"], pos + (2 * j + 2))
                    dve.tensor_tensor(ffn["hb"][:, :], bank(2, 2), c, ALU.mult).then_inc(s["gated"], 1)
                    dve.wait_ge(s["hid_hi"], g + 1)
                    dve.tensor_tensor(ffn["HL"][:, 2 * par + j, :], ffn["hb"][:, :], ffn["HH"][:, 2 * par + j, :],
                                      ALU.subtract).then_inc(s["hid_lo"], 1)

                def add_down(n, pos, last=False):
                    for m in range(KT):
                        g = 8 * n + (8 * GROUPS * layer + m)
                        if m < KT - 1:
                            dve.wait_ge(s["down_ready"], 7 * n + (7 * GROUPS * layer + m + 1))
                        else:
                            dve.wait_ge(s["blocks_freed"], pos + 2)
                        dve.tensor_tensor(X[:, m, :], X[:, m, :], bank(4 + 2 * (m % 2), 2), ALU.add).then_inc(
                            s["down_added"], 1)
                        if last and m:
                            add_square(2 * layer + 2, m - 1)
                    if last:
                        add_square(2 * layer + 2, KT - 1)

                params(0)
                for j in range(2):
                    tile(0, j, b0, 0)
                with dve.Fori(0, (GROUPS - 1) // 2) as i:
                    link.enter(i, links)
                    for q in range(2):
                        params(2 * i + (1 + q))
                        for j in range(2):
                            tile(2 * i + (1 + q), j, 12 * i + (b0 + 4 + 6 * q), (1 + q) % 2)
                        add_down(2 * i + q, 12 * i + (b0 + 8 + 6 * q))
                link.leave((GROUPS - 1) // 2)
                add_down(GROUPS - 1, b0 + 6 * GROUPS - 2, last=True)

            dve.wait_ge(s["rows_in"], 64)
            attention("f", fox, 1, H_FOX, 2 * NT)
            stage_end(dve, 4)
            out_projection(B_EVOUT, 0, 1)
            stage_end(dve, 5)
            norm(1)
            feed_forward(0, B_FFN0, 4)
            stage_end(dve, 6)
            norm(2)
            stage_end(dve, 7)
            dve.wait_ge(s["spilled"], 48)
            lam = lambda n: col(C_LAM + n * DH, DH)
            e = dif["xs"]
            link(dve.tensor_tensor(e[:, 0:DH], lam(0), lam(1), ALU.mult))
            link(dve.tensor_tensor(e[:, DH:2 * DH], lam(2), lam(3), ALU.mult))
            dve.tensor_reduce(small[:, 42:44], e[:, 0:2 * DH].rearrange("p (a b) -> p a b", a=2), AX.X, ALU.add).then_inc(
                s["rows_scan"], 1)
            dve.tensor_scalar(small[:, 40:41], col(C_SUBLN), 1.0 - LAMBDA_INIT, None, ALU.mult).then_inc(s["rows_scan"], 1)
            dve.wait_ge(s["rows_l"], 3)
            link(dve.tensor_tensor(small[:, 41:42], small[:, 45:46], small[:, 44:45], ALU.subtract))
            link(dve.tensor_scalar(small[:, 41:42], small[:, 41:42], -LAMBDA_INIT, None, ALU.add))
            attention("d", dif, 2, H_DIFF, 6 * NT)
            stage_end(dve, 8)
            out_projection(B_ODOUT, 8, 3)
            stage_end(dve, 9)
            norm(3)
            feed_forward(1, B_FFN1, 4)
            stage_end(dve, 10)
            norm(4)


def _constants():
    k, c = np.arange(P)[:, None], np.arange(P)[None, :]
    same = k // CHUNK == c // CHUNK
    out = {"ident": np.eye(P), "mask": np.where(c <= k, 0.0, NEG)}
    out["mi"] = np.where(same & (k <= c), 1.0, 0.0)
    out["lm"] = np.stack([np.where((k // (2 << v) == c // (2 << v)) & ((k >> v) % 2 == 0) & ((c >> v) % 2 == 1), -1.0, 0.0)
                          for v in range(LEVELS)], axis=1)
    rst = np.zeros((P, S))
    rst[R_G:R_F] = (np.arange(S) % CHUNK != 0)
    rst[R_F:] = 1.0
    out["rst"] = rst
    selg, selc = np.zeros((P, 4, P)), np.zeros((P, 4, P))
    for h in range(4):
        selg[R_G + h, h] = 1.0
        selc[R_F + h, h] = -1.0
        selc[R_TAIL + h, h] = -1.0
    out["selg"], out["selc"] = selg, selc
    half = DH // 2
    inv = (1.0 / (10000.0 ** (np.arange(half, dtype=np.float32) * 2.0 / DH))).astype(np.float32)
    ang = inv[:, None] * np.arange(S, dtype=np.float32)[None, :]
    out["cosT"] = np.tile(np.cos(ang), (4, 1))
    out["sinT"] = np.concatenate([-np.sin(ang), np.sin(ang)] * 2)
    return {n: np.ascontiguousarray(a, dtype=np.float32) for n, a in out.items()}


def _column_blocks(w):
    n = w.shape[1] // P
    return w.reshape(KT, P, n, P).transpose(2, 1, 0, 3).reshape(n, P, D)


def _layout(a):
    w_in = a["ev_w_in"][0]
    at = np.cumsum([0, 3 * H_DN * P, H_DN * P, H_DN, H_DN, H_FOX * P, H_FOX * P, H_FOX * P, H_FOX])
    part = lambda n: w_in[:, at[n]:at[n + 1]]
    logits = np.zeros((D, P), np.float32)
    for r, n in ((R_BETA, 2), (R_G, 3), (R_F, 7)):
        logits[:, r:r + 4] = part(n)
    per_head = lambda q, k, v: np.stack([q, k, v], axis=1).reshape(-1, P, D)
    blocks = [_column_blocks(logits), _column_blocks(part(0)), _column_blocks(part(1)),
              per_head(*(_column_blocks(part(n)) for n in (4, 5, 6))), _column_blocks(a["ev_w_out"][0])]

    def feed_forward(layer):
        gate, val = np.split(_column_blocks(a["ffn_w_up"][layer]), 2)
        down = a["ffn_w_down"][layer].reshape(FT, P, D)
        up = lambda n: [gate[2 * n], val[2 * n], gate[2 * n + 1], val[2 * n + 1]]
        order = up(0)
        for n in range(1, GROUPS):
            order += up(n) + [down[2 * n - 2], down[2 * n - 1]]
        return np.stack(order + [down[-2], down[-1]])

    blocks.append(feed_forward(0))
    blocks.append(per_head(*(np.split(_column_blocks(a["od_w_in"][0]), 3))))
    blocks.append(_column_blocks(a["od_w_out"][0]))
    blocks.append(feed_forward(1))
    w = np.concatenate(blocks)
    assert w.shape[0] == N_BLOCKS

    tiles = lambda v: v.reshape(-1, P).T
    cols = np.zeros((P, N_COLS), np.float32)
    for n, v in enumerate((a["ev_norm_w"][0], a["ffn_norm_w"][0], a["od_norm_w"][0], a["ffn_norm_w"][1],
                           a["final_norm_w"])):
        cols[:, C_NORM + KT * n:C_NORM + KT * (n + 1)] = tiles(v)
    cols[:, C_DNCONV:C_FFN] = a["dn_conv_w"][0].reshape(4, 12, P).transpose(2, 1, 0).reshape(P, 48)
    for layer in range(2):
        taps = np.concatenate([a["ffn_conv_w"][layer], a["ffn_conv_b"][layer][None]]).reshape(4, FT, P)
        cols[:, C_FFN + layer * FT * 4:C_FFN + (layer + 1) * FT * 4] = taps.transpose(2, 1, 0).reshape(P, FT * 4)
    cols[:, C_DNW] = a["dn_norm_w"][0]
    cols[:, C_SUBLN] = a["diff_subln_w"][0]
    cols[:, C_LAM:C_ROW] = a["diff_lambda"][0].reshape(1, 4 * DH)
    cols[:, C_ROW] = 0.0
    for r, sign, bias, alog in ((R_BETA, -1.0, None, None), (R_G, 1.0, a["dn_dt_bias"][0], a["dn_a_log"][0]),
                                (R_F, -1.0, a["fox_f_bias"][0], None)):
        cols[r:r + 4, C_ROW] = sign
        if bias is not None:
            cols[r:r + 4, C_ROW + 1] = bias
        if alog is not None:
            cols[r:r + 4, C_ROW + 2] = alog
    return {"w": w, "cols": cols, "xT": np.ascontiguousarray(a["x"][0].T), **_constants()}


def kernel(**inputs):
    import concourse.bacc as _bacc
    from concourse.bass_utils import run_bass_kernel_spmd as _run

    arrays = _layout({n: np.asarray(v) for n, v in inputs.items()})
    nc = _bacc.Bacc("TRN2", target_bir_lowering=False, num_devices=1)
    t = {n: nc.dram_tensor(f"in_{n}", a.shape, mybir.dt.from_np(a.dtype), kind="ExternalInput").ap()
         for n, a in arrays.items()}
    t["out"] = nc.dram_tensor("out_T", [D, S], F32, kind="ExternalOutput").ap()
    t["qkv"] = nc.dram_tensor("qkv_scratch", [12, P, S], F32, kind="Internal").ap()
    t["kept"] = nc.dram_tensor("projections_scratch", [KEPT, P, S], F32, kind="Internal").ap()
    t["spill"] = nc.dram_tensor("x_scratch", [D, S], F32, kind="Internal").ap()
    build(nc, t)
    r = _run(nc, [{f"in_{n}": a for n, a in arrays.items()}], core_ids=[0])
    return np.ascontiguousarray(r.results[0]["out_T"].T)[None]
```
